# Optimizing a Trainium2 kernel written in Bass

```python
import jax, jax.numpy as jnp
from jax import lax
import numpy as np

D_MODEL = 1024
BATCH = 1
SEQ = 512
DEPTH = 2

N_MIXERS = 2
MEM_LEN = 256
EPS = 1e-6
HG_HEADS = 8
HG_DIM = D_MODEL // HG_HEADS
HG_WIDTH = HG_HEADS * HG_DIM
HG_CHUNK = 64
GM_CHUNK = 128
GM_GROUPS = 8
GM_WIDTH = 2 * D_MODEL
GM_GROUP_DIM = GM_WIDTH // GM_GROUPS
XA_HEADS = 4
XA_DIM = D_MODEL // XA_HEADS
XA_WIDTH = XA_HEADS * XA_DIM
D_FF = 2816
N_HGRN = (DEPTH + 1) // 2
N_GMLP = DEPTH // 2
HG_IN = 4 * HG_WIDTH + XA_WIDTH
GM_IN = 2 * GM_WIDTH + XA_WIDTH

kernel_name = "hybrid_hgrn2_gmlp_memory_macaron"

def rmsnorm(x, g):
    xf = x.astype(jnp.float32)
    y = xf * lax.rsqrt(jnp.mean(xf * xf, axis=-1, keepdims=True) + EPS)
    return (y * g.astype(jnp.float32)).astype(x.dtype)

def layernorm(x, g, b):
    xf = x.astype(jnp.float32)
    mu = jnp.mean(xf, axis=-1, keepdims=True)
    xc = xf - mu
    y = xc * lax.rsqrt(jnp.mean(xc * xc, axis=-1, keepdims=True) + EPS)
    return (y * g.astype(jnp.float32) + b.astype(jnp.float32)).astype(x.dtype)

def swiglu_ffn(h, w_in, w_out):
    gate, up = jnp.split(h @ w_in, 2, axis=-1)
    return (jax.nn.silu(gate) * up) @ w_out

def memory_attention(zq, mem_k, mem_v):
    B, T, _ = zq.shape
    q = zq.reshape(B, T, XA_HEADS, XA_DIM)
    s = jnp.einsum('bthd,bmhd->bhtm', q, mem_k).astype(jnp.float32) * (XA_DIM ** -0.5)
    p = jax.nn.softmax(s, axis=-1).astype(mem_v.dtype)
    o = jnp.einsum('bhtm,bmhd->bthd', p, mem_v)
    return o.reshape(B, T, XA_WIDTH)

def hgrn2_recurrence(q, k, v, log_f):
    B, T, H, Dk = q.shape
    Dv = v.shape[-1]
    n = T // HG_CHUNK

    def to_chunks(a):
        return a.reshape(B, n, HG_CHUNK, H, a.shape[-1]).transpose(1, 0, 3, 2, 4)

    qc, kc, vc, lc = to_chunks(q), to_chunks(k), to_chunks(v), to_chunks(log_f)
    causal = jnp.tril(jnp.ones((HG_CHUNK, HG_CHUNK), dtype=bool))

    def step(S, inp):
        qn, kn, vn, ln = inp
        b = jnp.cumsum(ln, axis=2)
        b_last = b[:, :, -1:, :]
        q_dec = qn * jnp.exp(b)
        k_inv = kn * jnp.exp(-b)
        a = jnp.einsum('bhtk,bhsk->bhts', q_dec, k_inv)
        a = jnp.where(causal, a, 0.0)
        o = jnp.einsum('bhts,bhsv->bhtv', a, vn) + jnp.einsum('bhtk,bhkv->bhtv', q_dec, S)
        S_new = jnp.exp(b_last[:, :, 0, :])[..., None] * S + jnp.einsum(
            'bhsk,bhsv->bhkv', kn * jnp.exp(b_last - b), vn)
        return S_new, o

    S0 = jnp.zeros((B, H, Dk, Dv), jnp.float32)
    _, o = lax.scan(step, S0, (qc, kc, vc, lc))
    return o.transpose(1, 0, 3, 2, 4).reshape(B, T, H, Dv)

def hgrn2_mixer(zq, zf, zi, zg, lb, gnorm_g):
    B, T, _ = zq.shape
    shp = (B, T, HG_HEADS, HG_DIM)
    q = jax.nn.silu(zq.astype(jnp.float32)).reshape(shp)
    lbh = lb.astype(jnp.float32).reshape(HG_HEADS, HG_DIM)
    f = lbh + (1.0 - lbh) * jax.nn.sigmoid(zf.astype(jnp.float32).reshape(shp))
    k = 1.0 - f
    v = zi.astype(jnp.float32).reshape(shp)
    o = hgrn2_recurrence(q, k, v, jnp.log(f))
    o = rmsnorm(o, gnorm_g) * jax.nn.silu(zg.astype(jnp.float32).reshape(shp))
    return o.reshape(B, T, HG_WIDTH).astype(zq.dtype)

def chunked_spatial_gating(zu, zv, ln_g, ln_b, w_s, b_s):
    B, T, _ = zu.shape
    n = T // GM_CHUNK
    u = jax.nn.gelu(zu, approximate=False)
    v = layernorm(jax.nn.gelu(zv, approximate=False), ln_g, ln_b)
    vc = v.reshape(B, n, GM_CHUNK, GM_GROUPS, GM_GROUP_DIM)
    causal = jnp.tril(jnp.ones((GM_CHUNK, GM_CHUNK), dtype=bool))
    w = jnp.where(causal[None], w_s, 0.0).astype(v.dtype)
    mixed = jnp.einsum('gts,bnsgc->bntgc', w, vc) + b_s.T.astype(v.dtype)[None, None, :, :, None]
    return u * mixed.reshape(B, T, GM_WIDTH)

def setup_inputs(seed: int = 0) -> dict:
    key = jax.random.key(seed)
    ks = iter(jax.random.split(key, 32))

    def nrm(shape, scale):
        return jax.random.normal(next(ks), shape, jnp.float32) * scale

    def gain(shape):
        return 1.0 + nrm(shape, 0.05)

    return {
        "x": nrm((BATCH, SEQ, D_MODEL), 1.0),
        "mem": nrm((BATCH, MEM_LEN, D_MODEL), 1.0),
        "mem_norm": gain((D_MODEL,)),
        "lb_logits": nrm((DEPTH + 1, HG_WIDTH), 0.1),
        "ffn1_norm": gain((DEPTH, D_MODEL)),
        "ffn1_w_in": nrm((DEPTH, D_MODEL, 2 * D_FF), D_MODEL ** -0.5),
        "ffn1_w_out": nrm((DEPTH, D_FF, D_MODEL), D_FF ** -0.5),
        "mix_norm": gain((DEPTH, D_MODEL)),
        "mem_w_kv": nrm((DEPTH, D_MODEL, 2 * XA_WIDTH), D_MODEL ** -0.5),
        "hgrn_w_in": nrm((N_HGRN, D_MODEL, HG_IN), D_MODEL ** -0.5),
        "hgrn_gnorm": gain((N_HGRN, HG_DIM)),
        "hgrn_w_out": nrm((N_HGRN, HG_WIDTH + XA_WIDTH, D_MODEL), (HG_WIDTH + XA_WIDTH) ** -0.5),
        "gmlp_w_in": nrm((N_GMLP, D_MODEL, GM_IN), D_MODEL ** -0.5),
        "gmlp_ln_g": gain((N_GMLP, GM_WIDTH)),
        "gmlp_ln_b": nrm((N_GMLP, GM_WIDTH), 0.02),
        "gmlp_w_s": nrm((N_GMLP, GM_GROUPS, GM_CHUNK, GM_CHUNK), GM_CHUNK ** -0.5),
        "gmlp_b_s": 1.0 + nrm((N_GMLP, GM_GROUPS, GM_CHUNK), 0.1),
        "gmlp_w_out": nrm((N_GMLP, GM_WIDTH + XA_WIDTH, D_MODEL), (GM_WIDTH + XA_WIDTH) ** -0.5),
        "ffn2_norm": gain((DEPTH, D_MODEL)),
        "ffn2_w_in": nrm((DEPTH, D_MODEL, 2 * D_FF), D_MODEL ** -0.5),
        "ffn2_w_out": nrm((DEPTH, D_FF, D_MODEL), D_FF ** -0.5),
        "final_norm": gain((D_MODEL,)),
    }

def reference(x, mem, mem_norm, lb_logits, ffn1_norm, ffn1_w_in, ffn1_w_out, mix_norm, mem_w_kv,
              hgrn_w_in, hgrn_gnorm, hgrn_w_out, gmlp_w_in, gmlp_ln_g, gmlp_ln_b, gmlp_w_s, gmlp_b_s,
              gmlp_w_out, ffn2_norm, ffn2_w_in, ffn2_w_out, final_norm):
    B, T, _ = x.shape
    M = mem.shape[1]
    mem_n = rmsnorm(mem, mem_norm)
    lower_bounds = jnp.cumsum(jax.nn.softmax(lb_logits.astype(jnp.float32), axis=0), axis=0)

    for i in range(DEPTH):
        x = x + 0.5 * swiglu_ffn(rmsnorm(x, ffn1_norm[i]), ffn1_w_in[i], ffn1_w_out[i])

        h = rmsnorm(x, mix_norm[i])
        mk, mv = jnp.split(mem_n @ mem_w_kv[i], 2, axis=-1)
        mk = mk.reshape(B, M, XA_HEADS, XA_DIM)
        mv = mv.reshape(B, M, XA_HEADS, XA_DIM)
        j = i // N_MIXERS
        if i % N_MIXERS == 0:
            z = h @ hgrn_w_in[j]
            zq, zf, zi, zg, zx = jnp.split(z, [HG_WIDTH, 2 * HG_WIDTH, 3 * HG_WIDTH, 4 * HG_WIDTH], axis=-1)
            o_mix = hgrn2_mixer(zq, zf, zi, zg, lower_bounds[i], hgrn_gnorm[j])
            w_out = hgrn_w_out[j]
        else:
            z = h @ gmlp_w_in[j]
            zu, zv, zx = jnp.split(z, [GM_WIDTH, 2 * GM_WIDTH], axis=-1)
            o_mix = chunked_spatial_gating(zu, zv, gmlp_ln_g[j], gmlp_ln_b[j], gmlp_w_s[j], gmlp_b_s[j])
            w_out = gmlp_w_out[j]
        o_mem = memory_attention(zx, mk, mv)
        x = x + jnp.concatenate([o_mix, o_mem], axis=-1) @ w_out

        x = x + 0.5 * swiglu_ffn(rmsnorm(x, ffn2_norm[i]), ffn2_w_in[i], ffn2_w_out[i])

    return rmsnorm(x, final_norm)


_drawn_inputs = setup_inputs


def setup_inputs(seed=0):
    import zlib

    import numpy as np

    out = dict(_drawn_inputs(seed))
    spreads = {}
    factors = {'mem_norm': 8.0,
     'lb_logits': 49.357,
     'gmlp_ln_g': 18.53,
     'gmlp_ln_b': 46.871,
     'hgrn_gnorm': 5.54,
     'gmlp_b_s': 6.622,
     'ffn2_norm': 6.035}
    for name, (base, spread) in spreads.items():
        noise = np.random.default_rng([zlib.crc32(name.encode()), seed]).standard_normal(out[name].shape)
        drawn = base * np.exp(spread * noise) if base else spread * noise
        out[name] = __import__('jax').numpy.asarray(drawn.astype(out[name].dtype))
    for name, factor in factors.items():
        out[name] = (out[name] * factor).astype(out[name].dtype)
    return out
```

```python
from contextlib import ExitStack

import numpy as np

import concourse.bass as bass
from concourse import mybir
from concourse.alu_op_type import AluOpType as ALU

F32 = mybir.dt.float32
F32R = mybir.dt.float32r
I32 = mybir.dt.int32
ACT = mybir.ActivationFunctionType
AX_X = mybir.AxisListType.X

P = 128
EPS = 1e-6
D = 1024
DB = D // P
T = 512
MEM = 256
MB = MEM // P
FF = 2816
FB = FF // P
HEADS = 8
CHUNK = 64
NCH = T // CHUNK
TB = T // P
GW = 2048
GB = GW // P
GROUPS = 8
XH = 4
XSCALE = 256 ** -0.5
KU = 8
LANES = 4

ROWS = {}
_at = 0
for _name, _n in (("mem_norm", DB), ("ffn1_norm", 2 * DB), ("mix_norm", 2 * DB), ("ffn2_norm", 2 * DB),
                  ("final_norm", DB), ("lb_logits", 3 * DB), ("hgrn_gnorm", 1), ("gmlp_ln_g", GB),
                  ("gmlp_ln_b", GB)):
    ROWS[_name] = _at
    _at += _n
NROWS = _at
assert NROWS <= P


class Phase:

    quad = 0
    group = 0

    def __init__(self, units, groups):
        self.q0, self.g0 = Phase.quad, Phase.group
        self.units, self.groups = units, groups
        Phase.quad += units // LANES
        Phase.group += groups

    @property
    def end_quad(self):
        return self.q0 + self.units // LANES


def hybrid_trunk(nc, a, out):
    Phase.quad = Phase.group = 0
    kv = Phase(32, 32)
    phases = []
    for kind, units, groups in (("ffn_in", 44, 44), ("ffn_out", 24, 8), ("hgrn_in", 40, 40), ("hgrn_out", 16, 8),
                                ("ffn_in", 44, 44), ("ffn_out", 24, 8), ("ffn_in", 44, 44), ("ffn_out", 24, 8),
                                ("gmlp_in", 40, 40), ("gmlp_out", 24, 8), ("ffn_in", 44, 44), ("ffn_out", 24, 8)):
        phases.append((kind, Phase(units, groups)))
    LAST_QUAD = Phase.quad

    def blocks_of(w):
        return w.rearrange("(kb p) c -> p kb c", p=P)

    ffn_w = [(blocks_of(a[f"{n}_w_in"][i]), blocks_of(a[f"{n}_w_out"][i]))
             for i, n in ((0, "ffn1"), (0, "ffn2"), (1, "ffn1"), (1, "ffn2"))]
    hgrn_w = blocks_of(a["hgrn_w_in"][0]), blocks_of(a["hgrn_w_out"][0])
    gmlp_w = blocks_of(a["gmlp_w_in"][0]), blocks_of(a["gmlp_w_out"][0])
    kv_w = [blocks_of(a["mem_w_kv"][i]) for i in range(2)]
    OUT_ROWS = {"ffn_out": [(0, 0, 8), (8, 8, 8), (16, 16, FB - 16)],
                "hgrn_out": [(8, 16, 8), (0, 0, 8)],
                "gmlp_out": [(16, 16, 8), (0, 0, 8), (8, 8, 8)]}
    GAINS = [ROWS["ffn1_norm"], ROWS["mix_norm"], ROWS["ffn2_norm"],
             ROWS["ffn1_norm"] + DB, ROWS["mix_norm"] + DB, ROWS["ffn2_norm"] + DB, ROWS["final_norm"]]

    k_scratch = nc.dram_tensor("k_scratch", (32, P, MEM), F32).ap()
    v_scratch = nc.dram_tensor("v_scratch", (32, P, MEM), F32).ap()

    with ExitStack() as ctx:
        def sb(name, shape, dt=F32):
            return ctx.enter_context(nc.sbuf_tensor(name, shape, dt))

        sems = {}

        def sem(name):
            if name not in sems:
                sems[name] = ctx.enter_context(nc.semaphore(name))
            return sems[name]

        x = sb("x", [P, DB, T])
        raw = sb("raw", [P, LANES, KU, P])
        w_hi = sb("w_hi", [P, 2, KU, P], F32R)
        w_lo = sb("w_lo", [P, 2, KU, P], F32R)
        ident = sb("ident", [P, P])
        ones = sb("ones", [P, P])
        vecs = sb("vecs", [P, NROWS])
        rstd = sb("rstd", [P, T])
        sq = sb("sq", [P, 2, T])
        tmp = sb("tmp", [P, 6, T])
        pair = sb("pair", [P, 2, T])
        bs_all = sb("bs_all", [P, GROUPS, P])
        q_row = sb("q_row", [P, P])
        small = sb("small", [P, 96])
        with nc.sbuf_tensor("h_hi", [P, DB, T], F32R) as h_hi, nc.sbuf_tensor("h_lo", [P, DB, T], F32R) as h_lo:
            pass
        out_rows = sb("out_rows", [P, 2 * DB, T])[:, 0:DB, :].rearrange("p b t -> p (b t)").rearrange(
            "p (tb c) -> p tb c", tb=TB)
        with nc.sbuf_tensor("act_hi", [P, 24, T], F32R) as act_hi, nc.sbuf_tensor("act_lo", [P, 24, T], F32R) as act_lo:
            pass
        work = sb("work", [P, 48, T])

        acc = [ctx.enter_context(nc.psum_tensor(f"acc{i}", [P, T], F32)) for i in range(LANES)]
        mix = [ctx.enter_context(nc.psum_tensor(f"mix{i}", [P, T], F32)) for i in range(4)]

        sq_sum, sq_one = sq[:, 0, :], sq[:, 1, :]
        mem_hi = act_hi[:, 0:4, :].rearrange("p b (k m) -> p (b k) m", k=2)
        mem_lo = act_lo[:, 0:4, :].rearrange("p b (k m) -> p (b k) m", k=2)
        mem_raw = work[:, 40:44, :].rearrange("p b t -> p (b t)").rearrange("p (mb c) -> p mb c", mb=MB)
        mem_g = work[:, 44:48, :].rearrange("p b (k m) -> p (b k) m", k=2)
        mem_junk = work[:, 36:38, :].rearrange("p b t -> p (b t)")
        x_raw = work[:, 16:24, :].rearrange("p b t -> p (b t)").rearrange("p (tb c) -> p tb c", tb=TB)
        vec_rows = work[:, 38, 0:P]

        def f32(ap):
            return ap.bitcast(F32)

        def loop(eng, lo, hi, body):
            if hi - lo == 1:
                body(lo)
            else:
                with eng.Fori(lo, hi) as it:
                    body(it)

        def stand_alone(eng):
            eng.sem_inc(sem("wait_passed"), 1)

        def nxt(q, j):
            return (q, j + 1) if j + 1 < LANES else (q + 1, 0)

        w_loaded = [sem(f"w_loaded{j}") for j in range(LANES)]
        w_hi_ready, w_lo_ready = sem("w_hi_ready"), sem("w_lo_ready")
        unit_done = sem("unit_done")
        acc_read = sem("acc_read")
        xg_ready, h_hi_ready, h_lo_ready = sem("xg_ready"), sem("h_hi_ready"), sem("h_lo_ready")
        sq_ready, sq_sum_ready = sem("sq_ready"), sem("sq_sum_ready")
        ss_done, var_ready, std_ready, rstd_ready = (sem("ss_done"), sem("var_ready"), sem("std_ready"),
                                                     sem("rstd_ready"))
        silu_done, prod_done, act_hi_ready, act_lo_ready = (sem("silu_done"), sem("prod_done"), sem("act_hi_ready"),
                                                            sem("act_lo_ready"))

        class Attention:
            def __init__(self, layer, phase, kv_at, tmp_at):
                self.layer, self.ph = layer, phase
                self.kT = work[:, kv_at:kv_at + 4, :].rearrange("p b (k m) -> p (b k) m", k=2)
                self.v = work[:, kv_at + 4:kv_at + 8, :].rearrange("p b (k mb c) -> p (b k) mb c", k=2, mb=MB)
                self.qT = work[:, tmp_at:tmp_at + 4, :]
                self.p = work[:, tmp_at + 4:tmp_at + 6, :].rearrange("p b (k m) -> p (b k) m", k=2)
                self.pT = work[:, tmp_at + 6:tmp_at + 8, :]

            def load(self, pool):
                pool.wait_ge(unit_done, LANES * self.ph.q0)
                for j in range(LANES):
                    pool.wait_ge(sem(f"k_stored{j}"), 16 * 8)
                    pool.wait_ge(sem(f"kv_stored{j}"), 16 * 8)
                b = 16 * self.layer
                pool.dma_start(self.kT, k_scratch[b:b + DB].rearrange("b p m -> p b m")).then_inc(sem("kv_loaded"), 16)
                pool.dma_start(self.v.rearrange("p b mb c -> p b (mb c)"),
                               v_scratch[b + DB:b + 2 * DB].rearrange("b p m -> p b m")).then_inc(sem("kv_loaded"), 16)

            def tensor(self, pe, s):
                if s % 2 == 0 and 0 <= (s - 4) // 2 < XH and s >= 4:
                    h = (s - 4) // 2
                    n = XH * self.layer + h
                    pe.wait_ge(sem("pT_ready"), 2 * (n + 1))
                    for dv in range(2):
                        for mb in range(MB):
                            m = pe.matmul(mix[2 + dv][:], self.v[:, 2 * h + dv, mb, :], self.pT[:, mb, :],
                                          start=(mb == 0), stop=(mb == MB - 1))
                    m.then_inc(sem("pv_done"), 1)
                if s % 2 == 0 and s >= 2 and (s - 2) // 2 < XH:
                    h = (s - 2) // 2
                    n = XH * self.layer + h
                    if h == 0:
                        pe.wait_ge(sem("kv_loaded"), 32 * (self.layer + 1))
                    pe.wait_ge(acc_read, self.ph.g0 + 2 * h + 2)
                    if n:
                        pe.wait_ge(sem("exp_done"), TB * n)
                    for tb in range(TB):
                        for d in range(2):
                            m = pe.matmul(mix[tb // 2][:, (tb % 2) * MEM:(tb % 2 + 1) * MEM],
                                          self.qT[:, 2 * (h % 2) + d, tb * P:(tb + 1) * P],
                                          self.kT[:, 2 * h + d, :], start=(d == 0), stop=(d == 1))
                    m.then_inc(sem("scores_done"), 1)
                if s % 2 == 1 and s >= 3 and (s - 3) // 2 < XH:
                    h = (s - 3) // 2
                    n = XH * self.layer + h
                    pe.wait_ge(sem("p_ready"), TB * (n + 1))
                    if n:
                        pe.wait_ge(sem("o_mem_lo"), 2 * n)
                    for mb in range(MB):
                        for tb in range(TB):
                            m = pe.transpose(mix[2 + mb][:, tb * P:(tb + 1) * P],
                                             self.p[:, tb, mb * P:(mb + 1) * P], ident[:])
                    m.then_inc(sem("p_turned"), 1)

            def vector(self, dve, s):
                if 1 <= s <= 2 * XH:
                    u = s - 1
                    dve.wait_ge(unit_done, LANES * self.ph.q0 + u + 1)
                    if u >= 4:
                        dve.wait_ge(sem("scores_done"), XH * self.layer + u // 2 - 1)
                    dve.tensor_tensor(self.qT[:, u % 4, :], acc[u % LANES][:], rstd[:], ALU.mult).then_inc(acc_read, 1)
                if s % 2 == 1 and s >= 3 and (s - 3) // 2 < XH:
                    n = XH * self.layer + (s - 3) // 2
                    mx, neg, tot, inv = small[:, 0:4], small[:, 4:8], small[:, 8:12], small[:, 12:16]
                    dve.wait_ge(sem("scores_done"), n + 1)
                    for b in range(2):
                        dve.tensor_reduce(mx[:, 2 * b:2 * b + 2], mix[b][:].rearrange("p (k m) -> p k m", k=2), AX_X,
                                          ALU.max).then_inc(sem("max_done"), 1)
                    dve.wait_ge(sem("max_done"), 2 * (n + 1))
                    dve.tensor_scalar(neg, mx, -XSCALE, None, ALU.mult).then_inc(sem("neg_max_ready"), 1)
                    dve.wait_ge(sem("exp_done"), TB * (n + 1))
                    dve.reciprocal(inv, tot).then_inc(sem("inv_ready"), 1)
                    dve.wait_ge(sem("inv_ready"), n + 1)
                    for tb in range(TB):
                        dve.tensor_scalar(self.p[:, tb, :], self.p[:, tb, :], inv[:, tb:tb + 1], None,
                                          ALU.mult).then_inc(sem("p_ready"), 1)
                if s % 2 == 1 and s >= 5 and (s - 5) // 2 < XH:
                    h = (s - 5) // 2
                    n = XH * self.layer + h
                    for dv in range(2):
                        b = 16 + 2 * h + dv
                        dve.wait_ge(sem("o_mem_hi"), 2 * n + dv + 1)
                        dve.tensor_tensor(act_lo[:, b, :], mix[2 + dv][:], f32(act_hi[:, b, :]),
                                          ALU.subtract).then_inc(sem("o_mem_lo"), 1)

            def scalar(self, act, s):
                if s % 2 == 1 and s >= 5 and (s - 5) // 2 < XH:
                    h = (s - 5) // 2
                    n = XH * self.layer + h
                    act.wait_ge(sem("pv_done"), n + 1)
                    for dv in range(2):
                        act.activation(act_hi[:, 16 + 2 * h + dv, :], mix[2 + dv][:],
                                       ACT.Copy).then_inc(sem("o_mem_hi"), 1)
                if s % 2 == 1 and s >= 3 and (s - 3) // 2 < XH:
                    h = (s - 3) // 2
                    n = XH * self.layer + h
                    act.wait_ge(sem("neg_max_ready"), n + 1)
                    if n:
                        act.wait_ge(sem("p_turned"), n)
                    for tb in range(TB):
                        act.activation(self.p[:, tb, :], mix[tb // 2][:, (tb % 2) * MEM:(tb % 2 + 1) * MEM], ACT.Exp,
                                       bias=small[:, 4 + tb:5 + tb], scale=XSCALE,
                                       accum_out=small[:, 8 + tb:9 + tb]).then_inc(sem("exp_done"), 1)
                if s % 2 == 0 and s >= 4 and (s - 4) // 2 < XH:
                    h = (s - 4) // 2
                    n = XH * self.layer + h
                    act.wait_ge(sem("p_turned"), n + 1)
                    if n:
                        act.wait_ge(sem("pv_done"), n)
                    for mb in range(MB):
                        act.activation(self.pT[:, mb, :], mix[2 + mb][:], ACT.Copy).then_inc(sem("pT_ready"), 1)

        class Hgrn:
            def __init__(self, phase):
                self.ph = phase
                (self.q, self.k, self.b, self.eb, self.enb, self.qdec, self.kinv,
                 self.khat) = (work[:, 8 + i, :] for i in range(8))
                self.vT, self.sg, self.khat_t, self.v_t, self.a_m = (work[:, 32 + i, :] for i in range(5))
                self.state = work[:, 37:39, :].rearrange("p b t -> p (b t)")
                self.mask = pair[:, 0, :].bitcast(I32)
                self.restart = pair[:, 1, :]
                self.decay = small[:, 16:16 + NCH]
                self.lb = small[:, 24:32]
                self.one_less_lb = small[:, 32:40]

            def tensor(self, pe, h, j, finish):
                n = h - 1
                pairs = [slice(P * i, P * (i + 1)) for i in range(TB)]
                if j == 0:
                    pe.wait_ge(sem("khat_ready"), n + 1)
                    pe.wait_ge(sem("qdec_ready"), 2 * (n + 1))
                    if finish:
                        pe.wait_ge(sem("state_done"), (NCH - 1) * n)
                        pe.wait_ge(sem("o_scaled"), n)
                        pe.wait_ge(sem("o_log"), n)
                    else:
                        pe.wait_ge(sem("o_mem_lo"), 2 * XH)
                    for c in pairs:
                        m = pe.transpose(mix[0][:, c], self.khat[:, c], ident[:])
                    m.then_inc(sem("khat_turned"), 1)
                    pe.wait_ge(acc_read, self.ph.g0 + 2 * XH + LANES * h - 1)
                    for c in pairs:
                        m = pe.transpose(mix[1][:, c], self.vT[:, c], ident[:])
                    m.then_inc(sem("v_turned"), 1)
                    for i, c in enumerate(pairs):
                        m = pe.matmul(mix[2][:, c], self.kinv[:, c], self.qdec[:, c], start=True, stop=True)
                    m.then_inc(sem("a_done"), 1)
                if j == 1:
                    pe.wait_ge(sem("khat_t_ready"), n + 1)
                    pe.wait_ge(sem("v_t_ready"), n + 1)
                    for c in range(NCH - 1):
                        half, cols = slice(CHUNK * (c % 2), CHUNK * (c % 2 + 1)), pairs[c // 2]
                        bank = mix[3 * (c % 2)]
                        m = pe.matmul(bank[:, P * (c // 2):P * (c // 2 + 1)], self.khat_t[half, cols],
                                      self.v_t[half, cols], start=True, stop=True)
                    m.then_inc(sem("kv_done"), 1)
                    pe.wait_ge(sem("a_masked"), n + 1)
                    for i, c in enumerate(pairs):
                        pe.matmul(mix[1][:, c], self.v_t[:, c], self.a_m[:, c], start=(i == 0), stop=False,
                                  skip_group_check=True)
                if j == 2:
                    pe.wait_ge(sem("state_done"), (NCH - 1) * (n + 1))
                    for c in range(1, NCH):
                        cols = slice(CHUNK * c, CHUNK * (c + 1))
                        m = pe.matmul(mix[1][:, cols], self.state[:, P * (c - 1):P * c], self.qdec[:, cols],
                                      start=False, stop=(c == NCH - 1), skip_group_check=True)
                    m.then_inc(sem("o_done"), 1)
                if j == 3:
                    pe.wait_ge(sem("o_squared"), n + 1)
                    pe.matmul(mix[2][:], ones[:], tmp[:, 4, :], start=True, stop=True).then_inc(sem("oss_done"), 1)

            def unit_of(self, h, j):
                return LANES * (self.ph.q0 + 2 + h) + j

            def vector(self, dve, h, j, own, mixer, finish):
                n = h - 1
                if j == 0:
                    if mixer:
                        dve.wait_ge(sem("khat_ready"), n + 1)
                        dve.wait_ge(unit_done, self.unit_of(h, 0))
                        dve.tensor_tensor(tmp[:, 2, :], acc[3][:], rstd[:], ALU.mult).then_inc(acc_read, 1)
                    if finish:
                        dve.wait_ge(sem("o_rstd"), n)
                        dve.scalar_tensor_tensor(tmp[:, 5, :], mix[1][:], vecs[:, ROWS["hgrn_gnorm"]:ROWS["hgrn_gnorm"] + 1],
                                                 tmp[:, 5, :], ALU.mult, ALU.mult).then_inc(sem("o_scaled"), 1)
                    if mixer:
                        dve.wait_ge(sem("g_den"), n + 1)
                        dve.reciprocal(tmp[:, 3, :], tmp[:, 3, :]).then_inc(sem("g_sig"), 1)
                    if finish:
                        dve.wait_ge(sem("o_hi"), n)
                        dve.tensor_tensor(act_lo[:, h - 2, :], tmp[:, 4, :], f32(act_hi[:, h - 2, :]),
                                          ALU.subtract).then_inc(sem("o_lo"), 1)
                if j == 1:
                    if own:
                        dve.wait_ge(unit_done, self.unit_of(h, 1))
                        dve.tensor_tensor(tmp[:, 0, :], acc[0][:], rstd[:], ALU.mult).then_inc(acc_read, 1)
                    if mixer:
                        dve.wait_ge(sem("a_done"), n + 1)
                        stand_alone(dve)
                        dve.copy_predicated(self.a_m, self.mask, mix[2][:]).then_inc(sem("a_masked"), 1)
                    if own:
                        dve.wait_ge(sem("q_den"), h + 1)
                        dve.reciprocal(tmp[:, 1, :], tmp[:, 1, :]).then_inc(sem("q_sig"), 1)
                if j == 2:
                    if own:
                        dve.wait_ge(unit_done, self.unit_of(h, 2))
                        if mixer:
                            dve.wait_ge(sem("g_ready"), n + 1)
                        dve.tensor_tensor(tmp[:, 2, :], acc[1][:], rstd[:], ALU.mult).then_inc(acc_read, 1)
                    if mixer:
                        dve.wait_ge(sem("kv_done"), n + 1)
                        for c in range(NCH - 1):
                            dst = self.state[:, P * c:P * (c + 1)]
                            kv_c = mix[3 * (c % 2)][:, P * (c // 2):P * (c // 2 + 1)]
                            if c == 0:
                                dve.tensor_copy(dst, kv_c).then_inc(sem("state_done"), 1)
                            else:
                                dve.wait_ge(sem("state_done"), (NCH - 1) * n + c)
                                dve.scalar_tensor_tensor(dst, self.state[:, P * (c - 1):P * c], self.decay[:, c:c + 1],
                                                         kv_c, ALU.mult, ALU.add).then_inc(sem("state_done"), 1)
                    if own:
                        lb, one_less = bass.ds(24 + h, 1), bass.ds(32 + h, 1)
                        dve.wait_ge(sem("f_den"), h + 1)
                        dve.reciprocal(tmp[:, 3, :], tmp[:, 3, :]).then_inc(sem("f_sig"), 1)
                        dve.wait_ge(sem("f_sig"), h + 1)
                        dve.tensor_scalar(tmp[:, 3, :], tmp[:, 3, :], small[:, one_less], small[:, lb], ALU.mult,
                                          ALU.add).then_inc(sem("f_ready"), 1)
                if j == 3 and own:
                    dve.wait_ge(unit_done, self.unit_of(h, 3))
                    dve.tensor_tensor(self.vT, acc[2][:], rstd[:], ALU.mult).then_inc(acc_read, 1)
                    dve.wait_ge(sem("logf_ready"), h + 1)
                    dve.tensor_tensor_scan(self.b, self.restart, tmp[:, 2, :], 0.0, ALU.mult,
                                           ALU.add).then_inc(sem("b_ready"), 1)
                    dve.wait_ge(sem("b_ready"), h + 1)
                    b3 = self.b.rearrange("p (c t) -> p c t", t=CHUNK)
                    dve.tensor_tensor(tmp[:, 2, :].rearrange("p (c t) -> p c t", t=CHUNK),
                                      b3[:, :, CHUNK - 1:CHUNK].to_broadcast([P, NCH, CHUNK]), b3,
                                      ALU.subtract).then_inc(sem("rest_ready"), 1)
                    dve.wait_ge(sem("eb_ready"), h + 1)
                    dve.tensor_copy(self.decay.rearrange("p (c o) -> p c o", o=1),
                                    self.eb.rearrange("p (c t) -> p c t", t=CHUNK)[:, :, CHUNK - 1:CHUNK]).then_inc(sem("decay_ready"), 1)

            def scalar(self, act, h, j, own, mixer, finish):
                n = h - 1
                g_at = self.ph.g0 + 2 * XH + LANES * h
                if j == 0:
                    if finish:
                        act.wait_ge(sem("oss_done"), n)
                        act.activation(tmp[:, 5, :], mix[2][:], ACT.Ln, bias=small[:, 40:41],
                                       scale=1.0 / P).then_inc(sem("o_log"), 1)
                        act.wait_ge(sem("o_log"), n)
                        act.activation(tmp[:, 5, :], tmp[:, 5, :], ACT.Exp, scale=-0.5).then_inc(sem("o_rstd"), 1)
                    if mixer:
                        act.wait_ge(acc_read, g_at)
                        act.activation(tmp[:, 3, :], tmp[:, 2, :], ACT.Exp, scale=-1.0).then_inc(sem("g_exp"), 1)
                    if finish:
                        act.wait_ge(sem("o_gated"), n)
                        act.activation(act_hi[:, h - 2, :], tmp[:, 4, :], ACT.Copy).then_inc(sem("o_hi"), 1)
                if j == 1:
                    if own:
                        act.wait_ge(acc_read, g_at + 1)
                        act.activation(tmp[:, 1, :], tmp[:, 0, :], ACT.Exp, scale=-1.0).then_inc(sem("q_exp"), 1)
                    if mixer:
                        act.wait_ge(sem("khat_turned"), n + 1)
                        act.activation(self.khat_t, mix[0][:], ACT.Copy).then_inc(sem("khat_t_ready"), 1)
                        act.wait_ge(sem("v_turned"), n + 1)
                        act.activation(self.v_t, mix[1][:], ACT.Copy).then_inc(sem("v_t_ready"), 1)
                if j == 2 and own:
                    act.wait_ge(acc_read, g_at + 2)
                    act.activation(tmp[:, 3, :], tmp[:, 2, :], ACT.Exp, scale=-1.0).then_inc(sem("f_exp"), 1)
                    act.wait_ge(sem("f_ready"), h + 1)
                    act.activation(tmp[:, 2, :], tmp[:, 3, :], ACT.Ln).then_inc(sem("logf_ready"), 1)
                if j == 3:
                    if mixer:
                        act.wait_ge(sem("o_done"), n + 1)
                        if finish:
                            act.wait_ge(sem("o_lo"), n)
                        act.activation(tmp[:, 4, :], mix[1][:], ACT.Square).then_inc(sem("o_squared"), 1)
                    if own:
                        act.wait_ge(sem("b_ready"), h + 1)
                        act.activation(self.eb, self.b, ACT.Exp).then_inc(sem("eb_ready"), 1)
                        act.activation(self.enb, self.b, ACT.Exp, scale=-1.0).then_inc(sem("enb_ready"), 1)
                        act.wait_ge(sem("rest_ready"), h + 1)
                        act.activation(tmp[:, 2, :], tmp[:, 2, :], ACT.Exp).then_inc(sem("rest_exp"), 1)

            def pool(self, pool, h, j, own, mixer, finish):
                n = h - 1
                if j == 0:
                    if mixer:
                        pool.wait_ge(sem("g_exp"), n + 1)
                        stand_alone(pool)
                        pool.tensor_scalar(tmp[:, 3, :], tmp[:, 3, :], 1.0, None, ALU.add).then_inc(sem("g_den"), 1)
                    if finish:
                        pool.wait_ge(sem("g_ready"), n)
                        pool.wait_ge(sem("o_scaled"), n)
                        pool.tensor_tensor(tmp[:, 4, :], tmp[:, 5, :], self.sg, ALU.mult).then_inc(sem("o_gated"), 1)
                    if mixer:
                        pool.wait_ge(sem("g_sig"), n + 1)
                        if finish:
                            pool.wait_ge(sem("o_gated"), n)
                        pool.tensor_tensor(self.sg, tmp[:, 2, :], tmp[:, 3, :], ALU.mult).then_inc(sem("g_ready"), 1)
                if j == 1 and own:
                    pool.wait_ge(sem("q_exp"), h + 1)
                    stand_alone(pool)
                    pool.tensor_scalar(tmp[:, 1, :], tmp[:, 1, :], 1.0, None, ALU.add).then_inc(sem("q_den"), 1)
                    pool.wait_ge(sem("q_sig"), h + 1)
                    pool.tensor_tensor(self.q, tmp[:, 0, :], tmp[:, 1, :], ALU.mult).then_inc(sem("q_ready"), 1)
                if j == 2 and own:
                    pool.wait_ge(sem("f_exp"), h + 1)
                    stand_alone(pool)
                    pool.tensor_scalar(tmp[:, 3, :], tmp[:, 3, :], 1.0, None, ALU.add).then_inc(sem("f_den"), 1)
                    pool.wait_ge(sem("f_ready"), h + 1)
                    stand_alone(pool)
                    pool.tensor_scalar(self.k, tmp[:, 3, :], -1.0, 1.0, ALU.mult, ALU.add).then_inc(sem("k_ready"), 1)
                if j == 3 and own:
                    if mixer:
                        pool.wait_ge(sem("o_done"), n + 1)
                    pool.wait_ge(sem("k_ready"), h + 1)
                    pool.wait_ge(sem("eb_ready"), h + 1)
                    pool.wait_ge(sem("q_ready"), h + 1)
                    pool.tensor_tensor(self.qdec, self.q, self.eb, ALU.mult).then_inc(sem("qdec_ready"), 1)
                    pool.wait_ge(sem("enb_ready"), h + 1)
                    pool.tensor_tensor(self.kinv, self.k, self.enb, ALU.mult).then_inc(sem("qdec_ready"), 1)
                    pool.wait_ge(sem("rest_exp"), h + 1)
                    pool.tensor_tensor(self.khat, self.k, tmp[:, 2, :], ALU.mult).then_inc(sem("khat_ready"), 1)

        class Gmlp:
            def __init__(self, phase):
                self.ph = phase
                self.w_raw = work[:, 14:16, :].rearrange("p b (k s) -> p (b k) s", s=P)
                self.w_turned = pair[:].rearrange("p b (k s) -> p (b k) s", s=P)
                self.row_sums = sq[:].rearrange("p b (k s) -> p (b k) s", s=P)
                self.mean_var = small[:, 48:56].rearrange("p (n z) -> p n z", z=2)
                self.v_rstd = small[:, 56:60]

            def setup_pool(self, pool):
                pool.wait_ge(unit_done, LANES * self.ph.q0)
                pool.dma_start(self.w_raw, a["gmlp_w_s"][0].rearrange("g t s -> t g s")).then_inc(sem("ws_loaded"), 16)
                pool.dma_start(bs_all[:], a["gmlp_b_s"][0:1].to_broadcast([P, GROUPS, P])).then_inc(sem("bs_loaded"), 16)
                pool.wait_ge(sem("ws_loaded"), 16)
                pool.affine_select(out=self.w_raw, in_=self.w_raw, compare_op=ALU.is_ge, fill=0.0, base=0,
                                   pattern=[[0, GROUPS], [-1, P]], channel_multiplier=1).then_inc(sem("ws_masked"), 1)

            def setup_tensor(self, pe, s):
                if s == 1:
                    pe.wait_ge(sem("ws_masked"), 1)
                    for g in range(GROUPS):
                        m = pe.transpose(mix[g // 4][:, P * (g % 4):P * (g % 4 + 1)], self.w_raw[:, g, :], ident[:])
                    m.then_inc(sem("ws_turned"), 1)
                if s == 2:
                    pe.wait_ge(sem("wt_ready"), 2)
                    for b in range(2):
                        m = pe.matmul(mix[2 + b][:], ones[:], pair[:, b, :], start=True, stop=True)
                    m.then_inc(sem("row_sums_done"), 1)
                if s == 3:
                    pe.wait_ge(sem("row_sums_ready"), 2)

            def setup_vector(self, dve, s):
                if s == 2:
                    dve.wait_ge(sem("ws_turned"), 1)
                    for b in range(2):
                        dve.tensor_copy(pair[:, b, :], mix[b][:]).then_inc(sem("wt_ready"), 1)
                if s == 3:
                    dve.wait_ge(sem("row_sums_done"), 1)
                    for b in range(2):
                        dve.tensor_copy(sq[:, b, :], mix[2 + b][:]).then_inc(sem("row_sums_ready"), 1)

            def v_tensor(self, pe, it, j, first=False):
                if first and j == 0:
                    return
                c = LANES * it + j
                b = (j - 1) % 2
                pe.wait_ge(sem("v_gelu"), c)
                if not first or j == 3:
                    pe.wait_ge(sem("v_stored"), c - 2)
                for n in range(TB):
                    m = pe.transpose(mix[b][:, P * n:P * (n + 1)], tmp[:, b, P * n:P * (n + 1)], ident[:])
                m.then_inc(sem("v_blk_turned"), 1)

            def v_vector(self, dve, it, j, first=False):
                c = LANES * it + j
                if not (first and j == 0):
                    b = (j - 1) % 2
                    dve.wait_ge(unit_done, LANES * (self.ph.q0 + 2) + c)
                    if not first or j == 3:
                        dve.wait_ge(sem("v_blk_turned"), c - 2)
                    dve.tensor_tensor(tmp[:, b, :], acc[(j - 1) % LANES][:], rstd[:], ALU.mult).then_inc(acc_read, 1)

            def v_stats(self, dve, it, j):
                if j >= 2:
                    dve.wait_ge(sem("v_stored"), LANES * it)
                    for n in (2 * j - 4, 2 * j - 3):
                        dve.bn_stats(v_stats_sb[:, n, it - 1, :], work[:, bass.ds(LANES * (it - 1), LANES), P * n:P * (n + 1)]
                                     ).then_inc(sem("v_stats"), 1)

            def v_stats_end(self, dve):
                dve.wait_ge(sem("v_stats"), 4 * TB)
                for n in range(TB):
                    dve.bn_aggr(self.mean_var[:, n, :], v_stats_sb[:, n, :, :]).then_inc(sem("v_aggr"), 1)
                dve.wait_ge(sem("v_aggr"), TB)
                dve.tensor_scalar(self.v_rstd.rearrange("p (n z) -> p n z", z=1), self.mean_var[:, :, 1:2], EPS, None,
                                  ALU.add).then_inc(sem("v_var"), 1)
                dve.wait_ge(sem("v_std"), 1)
                dve.reciprocal(self.v_rstd, self.v_rstd).then_inc(sem("v_rstd"), 1)

            def v_scalar(self, act, it, j, first=False):
                c = LANES * it + j
                if not (first and j < 2):
                    act.wait_ge(sem("v_blk_turned"), c - 1)
                    act.activation(work[:, c - 2, :], mix[(j - 2) % 2][:], ACT.Copy).then_inc(sem("v_stored"), 1)
                if not (first and j < 1):
                    act.wait_ge(acc_read, self.ph.g0 + 2 * XH + c)
                    b = (j - 1) % 2
                    act.activation(tmp[:, b, :], tmp[:, b, :], ACT.Gelu).then_inc(sem("v_gelu"), 1)

            def u_vector(self, dve, it, j):
                c = LANES * it + j
                dve.wait_ge(unit_done, LANES * (self.ph.q0 + 6) + c + 1)
                if type(it) is not int or c >= 2:
                    dve.wait_ge(sem("u_ready"), c - 1)
                else:
                    dve.wait_ge(sem("v_blk_turned"), GB)
                dve.tensor_tensor(tmp[:, j % 2, :], acc[j][:], rstd[:], ALU.mult).then_inc(acc_read, 1)

            def u_scalar(self, act, it, j):
                c = LANES * it + j
                act.wait_ge(acc_read, self.ph.g0 + 2 * XH + GB + c + 1)
                act.activation(work[:, 24 + c, :], tmp[:, j % 2, :], ACT.Gelu).then_inc(sem("u_ready"), 1)

            def norm_vector(self, dve, bt, j):
                m = LANES * bt + j
                if type(bt) is not int or m >= 2:
                    dve.wait_ge(sem("mixing_done"), m - 1)
                if type(bt) is int and m == 0:
                    dve.wait_ge(sem("v_rstd"), 1)
                for n in range(TB):
                    dve.tensor_scalar(tmp[:, 2 + j % 2, P * n:P * (n + 1)], work[:, m, P * n:P * (n + 1)],
                                      self.mean_var[:, n, 0:1], self.v_rstd[:, n:n + 1], ALU.subtract,
                                      ALU.mult).then_inc(sem("v_normed"), 1)

            def mix_tensor(self, pe, bt, j):
                m = LANES * bt + j
                pe.wait_ge(sem("v_normed"), TB * (m + 1))
                if type(bt) is not int or m >= 2:
                    pe.wait_ge(sem("mixed_ready"), m - 1)
                for n in range(TB):
                    mm = pe.matmul(mix[j % 2][:, P * n:P * (n + 1)], tmp[:, 2 + j % 2, P * n:P * (n + 1)],
                                   self.w_turned[:, 2 * bt + j // 2, :], start=True, stop=True)
                mm.then_inc(sem("mixing_done"), 1)

            def mix_vector(self, dve, bt, j):
                m, g = LANES * bt + j, 2 * bt + j // 2
                if type(bt) is int and m == 0:
                    dve.wait_ge(sem("bs_loaded"), 16)
                else:
                    dve.wait_ge(sem("mixed_ready"), m)
                dve.scalar_tensor_tensor(q_row[:], self.row_sums[:, g, :], vecs[:, bass.ds(ROWS["gmlp_ln_b"] + m, 1)],
                                         bs_all[:, g, :], ALU.mult, ALU.add).then_inc(sem("q_row_ready"), 1)
                dve.wait_ge(sem("q_row_ready"), m + 1)
                dve.wait_ge(sem("mixing_done"), m + 1)
                t = tmp[:, 4 + j % 2, :]
                dve.scalar_tensor_tensor(t.rearrange("p (n t) -> p n t", n=TB),
                                         mix[j % 2][:].rearrange("p (n t) -> p n t", n=TB),
                                         vecs[:, bass.ds(ROWS["gmlp_ln_g"] + m, 1)],
                                         q_row[:].rearrange("p (o t) -> p o t", o=1).to_broadcast([P, TB, P]),
                                         ALU.mult, ALU.add).then_inc(sem("mixed_ready"), 1)
                dve.wait_ge(sem("mix_hi"), m + 1)
                dve.tensor_tensor(act_lo[:, m, :], t, f32(act_hi[:, m, :]), ALU.subtract).then_inc(sem("mix_lo"), 1)

            def mix_pool(self, pool, bt, j):
                m = LANES * bt + j
                pool.wait_ge(sem("mixed_ready"), m + 1)
                pool.wait_ge(sem("u_ready"), m + 1)
                t = tmp[:, 4 + j % 2, :]
                pool.tensor_tensor(t, t, work[:, 24 + m, :], ALU.mult).then_inc(sem("mix_prod"), 1)

            def mix_scalar(self, act, bt, j):
                m = LANES * bt + j
                act.wait_ge(sem("mix_prod"), m + 1)
                act.activation(act_hi[:, m, :], tmp[:, 4 + j % 2, :], ACT.Copy).then_inc(sem("mix_hi"), 1)

        v_stats_sb = sb("v_stats_sb", [P, TB, 4, 6])
        in_phases = [i for i, (kind, _) in enumerate(phases) if kind.endswith("_in")]
        mixes = {}
        for i, (kind, ph) in enumerate(phases):
            if kind == "hgrn_in":
                mixes[i] = (Attention(0, ph, 0, 24), Hgrn(ph))
            if kind == "gmlp_in":
                mixes[i] = (Attention(1, ph, 24, 32), Gmlp(ph))

        block = ctx.enter_context(nc.Block())

        @block.sync
        def _(sp):
            sp.dma_start(mem_raw, a["mem"][0].rearrange("(mb p) c -> p mb c", p=P)).then_inc(sem("mem_loaded"), 16)

            def load(q, j, src, nkb=KU, fresh=False):
                if not fresh:
                    sp.wait_ge(w_lo_ready, LANES * q + j - 3)
                    stand_alone(sp)
                sp.dma_start(raw[:, j, 0:nkb, :], src).then_inc(w_loaded[j], 16)

            def cols(block):
                return bass.ds(block * P, P)

            for layer in range(2):
                def kv_body(it, fresh=False):
                    for j in range(LANES):
                        load(4 * layer + it, j, kv_w[layer][:, :, cols(LANES * it + j)], fresh=fresh)
                if layer == 0:
                    kv_body(0, fresh=True)
                loop(sp, 1 - layer, 4, kv_body)

            n_ffn = 0
            for kind, ph in phases:
                if kind == "ffn_in":
                    w = ffn_w[n_ffn][0]

                    def body(it):
                        for j in range(LANES):
                            load(ph.q0 + it, j, w[:, :, cols((j % 2) * FB + 2 * it + j // 2)])
                    loop(sp, 0, FB // 2, body)
                elif kind == "hgrn_in":
                    w = hgrn_w[0]

                    def body(it):
                        for j in range(LANES):
                            load(ph.q0 + it, j, w[:, :, cols(4 * DB + LANES * it + j)])
                    loop(sp, 0, 2, body)

                    def body(h):
                        for j in range(LANES):
                            load(ph.q0 + 2 + h, j, w[:, :, cols(DB * j + h)])
                    loop(sp, 0, HEADS, body)
                elif kind == "gmlp_in":
                    w = gmlp_w[0]
                    for first_quad, quads, at in ((0, 2, 2 * GB), (2, 4, GB), (6, 4, 0)):
                        def body(it):
                            for j in range(LANES):
                                load(ph.q0 + first_quad + it, j, w[:, :, cols(at + LANES * it + j)])
                        loop(sp, 0, quads, body)
                else:
                    w = (ffn_w[n_ffn] if kind == "ffn_out" else hgrn_w if kind == "hgrn_out" else gmlp_w)[1]
                    rows = OUT_ROWS[kind]

                    def body(it):
                        for r, (w0, _, nkb) in enumerate(rows):
                            for g in range(LANES):
                                load(ph.q0 + len(rows) * it + r, g, w[:, w0:w0 + nkb, cols(LANES * it + g)], nkb)
                    loop(sp, 0, 2, body)
                    n_ffn += kind == "ffn_out"
            out_v = out[0].rearrange("(tb p) c -> p tb c", p=P)
            for tb in range(TB):
                sp.wait_ge(sem("rows_by_vector" if tb % 2 == 0 else "rows_by_scalar"), tb // 2 + 1)
                sp.dma_start(out_v[:, tb, :], out_rows[:, tb, :]).then_inc(sem("stored"), 16)
            sp.wait_ge(sem("stored"), 16 * TB)

        @block.tensor
        def _(pe):
            pe.wait_ge(sem("consts"), 4)
            pe.wait_ge(sem("rows_loaded"), 16 * 9)
            pe.transpose(mix[3][:, 0:NROWS], vec_rows[0:NROWS, :], ident[0:NROWS, 0:NROWS]).then_inc(sem("vecs_turned"), 1)
            pe.wait_ge(sem("mem_normed"), MB)
            for kb in range(DB):
                if kb == 6:
                    pe.wait_ge(sem("vecs_ready"), 1)
                for mb in range(MB):
                    m = pe.transpose(mix[kb // 2][:, (kb % 2) * MEM + mb * P:(kb % 2) * MEM + (mb + 1) * P],
                                     mem_raw[:, mb, kb * P:(kb + 1) * P], ident[:])
                if kb % 2:
                    m.then_inc(sem("mem_turned"), 1)
            pe.wait_ge(sem("x_loaded"), 16)
            for m_ in range(DB):
                if m_ == LANES:
                    pe.wait_ge(sem("mem_gained"), DB)
                bank = acc[m_] if m_ < LANES else mix[m_ - LANES]
                for tb in range(TB):
                    m = pe.transpose(bank[:, tb * P:(tb + 1) * P], x_raw[:, tb, m_ * P:(m_ + 1) * P], ident[:])
                m.then_inc(sem("x_turned"), 1)

            def unit(q, j, operands, bank, start, stop, each=None):
                pe.wait_ge(w_lo_ready, LANES * q + j + 1)
                w = j % 2
                last = len(operands) - 1
                for i, (hi, lo) in enumerate(operands):
                    if each:
                        each(i)
                    pe.matmul(bank, w_hi[:, w, i, :], hi, start=(start and i == 0), stop=False)
                    pe.matmul(bank, w_hi[:, w, i, :], lo, start=False, stop=False)
                    m = pe.matmul(bank, w_lo[:, w, i, :], hi, start=False, stop=(stop and i == last))
                m.then_inc(unit_done, 1)

            mem_parts = [(mem_hi[:, k, :], mem_lo[:, k, :]) for k in range(DB)]

            def kv_turn(q, j, first=False):
                n = LANES * q + j
                pe.wait_ge(acc_read, n + 1)
                if not first:
                    pe.wait_ge(sem("v_staged"), n - 3)
                for mb in range(MB):
                    m = pe.transpose(mix[j][:, mb * P:(mb + 1) * P], tmp[:, j, mb * P:(mb + 1) * P], ident[:])
                m.then_inc(sem("kv_turned"), 1)

            def kv_body(it, first=False):
                for j in range(LANES):
                    if first and j == 0:
                        pe.wait_ge(sem("mem_lo_ready"), 1)
                        pe.wait_ge(sem("x_ready"), DB)
                    if not first:
                        pe.wait_ge(acc_read, LANES * it + j - 3)
                    unit(it, j, mem_parts, acc[j][:, 0:MEM], True, True)
                    if j:
                        kv_turn(it, j - 1, first)
                    elif not first:
                        kv_turn(it - 1, 3, False) if type(it) is not int or it > 1 else kv_turn(0, 3, True)

            kv_body(0, first=True)
            kv_body(1)
            loop(pe, 2, 8, kv_body)
            kv_turn(7, 3)

            h_parts = [(h_hi[:, k, :], h_lo[:, k, :]) for k in range(DB)]

            def in_unit(ph, s, it, j, first=False):
                def each(i):
                    pe.wait_ge(h_lo_ready, DB * s + i + 1)
                pe.wait_ge(acc_read, ph.g0 + LANES * it + j - 3)
                unit(ph.q0 + it, j, h_parts, acc[j][:], True, True, each if first and j == 0 else None)
                if first and j == 0:
                    if s == 0:
                        pe.wait_ge(sem("v_staged"), 32)
                    pe.wait_ge(sq_sum_ready, DB * (s + 1))
                    pe.matmul(mix[3][:], ones[:], sq_sum, start=True, stop=True).then_inc(ss_done, 1)

            s = n_ffn = 0
            for i, (kind, ph) in enumerate(phases):
                if kind == "ffn_in":
                    def body(it, first=False):
                        for j in range(LANES):
                            in_unit(ph, s, it, j, first)
                    body(0, first=True)
                    loop(pe, 1, FB // 2, body)
                elif kind == "hgrn_in":
                    att, hg = mixes[i]
                    for u in range(12):
                        in_unit(ph, s, u // LANES, u % LANES, first=(u == 0))
                        att.tensor(pe, u)

                    def body(h, finish=True):
                        for j in range(LANES):
                            in_unit(ph, s, 2 + h, j)
                            hg.tensor(pe, h, j, finish)
                    body(1, finish=False)
                    loop(pe, 2, HEADS, body)
                elif kind == "gmlp_in":
                    att, gm = mixes[i]
                    for u in range(12):
                        in_unit(ph, s, u // LANES, u % LANES, first=(u == 0))
                        gm.setup_tensor(pe, u)
                        if u >= 8:
                            gm.v_tensor(pe, 0, u - 8, first=True)
                        att.tensor(pe, u)

                    def v_body(it):
                        for j in range(LANES):
                            in_unit(ph, s, 2 + it, j)
                            gm.v_tensor(pe, it, j)
                    loop(pe, 1, 4, v_body)
                    for j in range(LANES):
                        in_unit(ph, s, 6, j)
                        if j == 0:
                            gm.v_tensor(pe, 4, 0)

                    def u_body(it):
                        for j in range(LANES):
                            in_unit(ph, s, 6 + it, j)
                            gm.mix_tensor(pe, it - 1, j)
                    u_body(1)
                    loop(pe, 2, 4, u_body)
                else:
                    rows = OUT_ROWS[kind]

                    def body(it, beside=None):
                        for r, (_, a0, nkb) in enumerate(rows):
                            parts = [(act_hi[:, a0 + k, :], act_lo[:, a0 + k, :]) for k in range(nkb)]
                            for g in range(LANES):
                                def each(k):
                                    if kind == "ffn_out":
                                        pe.wait_ge(act_lo_ready, FB * n_ffn + a0 + k + 1)
                                    elif a0 == 16:
                                        pe.wait_ge(sem("o_mem_lo"), 2 * XH * (n_ffn // 2 + 1))
                                    elif kind == "hgrn_out":
                                        pe.wait_ge(sem("o_lo"), k + 1)
                                    else:
                                        pe.wait_ge(sem("mix_lo"), a0 + k + 1)
                                if r == 0:
                                    pe.wait_ge(acc_read, ph.g0 + LANES * it + g - 3)
                                unit(ph.q0 + len(rows) * it + r, g, parts, acc[g][:], r == 0, r == len(rows) - 1,
                                     each if g == 0 and (beside is not None or kind == "ffn_out") else None)
                                if beside and r == 0:
                                    beside(g)
                                if s == len(in_phases) and r == len(rows) - 1:
                                    turn_out(it, g)

                    def turn_out(it, g):
                        for gg in ([g - 1] if g else []) + ([g] if g == LANES - 1 else []):
                            m_ = LANES * it + gg
                            pe.wait_ge(xg_ready, DB * s + m_ + 1)
                            for tb in range(TB):
                                m = pe.transpose(mix[gg][:, tb * P:(tb + 1) * P], tmp[:, 4 + gg % 2, tb * P:(tb + 1) * P],
                                                 ident[:])
                            m.then_inc(sem("out_turned"), 1)

                    s += 1
                    if kind == "hgrn_out":
                        hg = mixes[i - 1][1]
                        body(0, beside=lambda g: hg.tensor(pe, HEADS, g, True))
                        body(1)
                    elif kind == "gmlp_out":
                        gm = mixes[i - 1][1]
                        body(0, beside=lambda g: gm.mix_tensor(pe, 3, g))
                        body(1)
                    else:
                        if s == len(in_phases):
                            body(0)
                            pe.wait_ge(sem("out_staged"), LANES)
                            body(1)
                        else:
                            loop(pe, 0, 2, body)
                        n_ffn += 1
                    continue
            pe.wait_ge(sq_sum_ready, DB * (s + 1))
            pe.wait_ge(acc_read, Phase.group)
            for tb in range(TB):
                m = pe.matmul(acc[0][:, tb:tb + 1], sq_sum[:, tb * P:(tb + 1) * P], ones[:, 0:1], start=True, stop=True)
            m.then_inc(ss_done, 1)

        @block.vector
        def _(dve):
            def lo(q, j):
                dve.wait_ge(w_hi_ready, LANES * q + j + 1)
                dve.tensor_tensor(w_lo[:, j % 2], raw[:, j], f32(w_hi[:, j % 2]), ALU.subtract).then_inc(w_lo_ready, 1)

            dve.wait_ge(sem("mem_squared"), MB)
            mss = small[:, 60:62]
            dve.tensor_scalar(mss, mss, 1.0 / D, EPS, ALU.mult, ALU.add).then_inc(sem("mem_var"), 1)
            dve.wait_ge(sem("mem_std"), 1)
            dve.reciprocal(mss, mss).then_inc(sem("mem_rstd"), 1)
            dve.wait_ge(sem("mem_rstd"), 1)
            for mb in range(MB):
                dve.tensor_scalar(mem_raw[:, mb, :], mem_raw[:, mb, :], mss[:, mb:mb + 1], None,
                                  ALU.mult).then_inc(sem("mem_normed"), 1)
            dve.wait_ge(sem("vecs_turned"), 1)
            dve.tensor_copy(vecs[:], mix[3][:, 0:NROWS]).then_inc(sem("vecs_ready"), 1)
            dve.wait_ge(sem("vecs_ready"), 1)
            for kb in range(DB):
                dve.wait_ge(sem("mem_turned"), kb // 2 + 1)
                g = ROWS["mem_norm"] + kb
                dve.tensor_scalar(mem_g[:, kb, :], mix[kb // 2][:, (kb % 2) * MEM:(kb % 2 + 1) * MEM], vecs[:, g:g + 1],
                                  None, ALU.mult).then_inc(sem("mem_gained"), 1)
            for m_ in range(LANES):
                dve.wait_ge(sem("x_turned"), m_ + 1)
                dve.tensor_copy(x[:, m_, :], acc[m_][:]).then_inc(sem("x_ready"), 1)
            dve.wait_ge(sem("mem_hi_ready"), 1)
            dve.tensor_tensor(mem_lo, mem_g, f32(mem_hi), ALU.subtract).then_inc(sem("mem_lo_ready"), 1)
            lo(0, 0)
            for m_ in range(LANES, DB):
                dve.wait_ge(sem("x_turned"), m_ + 1)
                dve.tensor_copy(x[:, m_, :], mix[m_ - LANES][:]).then_inc(sem("x_ready"), 1)
            lg = [vecs[:, ROWS["lb_logits"] + DB * i:ROWS["lb_logits"] + DB * (i + 1)] for i in range(3)]
            top, e = small[:, 64:72], [small[:, 72 + 8 * i:80 + 8 * i] for i in range(3)]
            dve.tensor_tensor(top, lg[0], lg[1], ALU.max).then_inc(sem("lb_step"), 1)
            dve.wait_ge(sem("lb_step"), 1)
            dve.tensor_tensor(top, top, lg[2], ALU.max).then_inc(sem("lb_step"), 1)
            dve.wait_ge(sem("lb_step"), 2)
            for i in range(3):
                dve.tensor_tensor(e[i], lg[i], top, ALU.subtract).then_inc(sem("lb_shifted"), 1)
            dve.wait_ge(sem("lb_exp"), 1)
            dve.tensor_tensor(top, e[0], e[1], ALU.add).then_inc(sem("lb_step"), 1)
            dve.wait_ge(sem("lb_step"), 3)
            dve.tensor_tensor(top, top, e[2], ALU.add).then_inc(sem("lb_step"), 1)
            dve.wait_ge(sem("lb_step"), 4)
            dve.reciprocal(top, top).then_inc(sem("lb_step"), 1)
            dve.wait_ge(sem("lb_step"), 5)
            dve.tensor_tensor(small[:, 24:32], e[0], top, ALU.mult).then_inc(sem("lb_step"), 1)
            dve.wait_ge(sem("lb_step"), 6)
            dve.tensor_scalar(small[:, 32:40], small[:, 24:32], -1.0, 1.0, ALU.mult, ALU.add).then_inc(sem("lb_step"), 1)
            dve.wait_ge(sem("lb_step"), 7)

            def gained(s, m_, t):
                g = GAINS[s] + m_
                dve.tensor_scalar(t, x[:, m_, :], vecs[:, bass.ds(g, 1)], None, ALU.mult).then_inc(xg_ready, 1)

            def h_rest(s, m_, t):
                dve.wait_ge(h_hi_ready, DB * s + m_ + 1)
                dve.tensor_tensor(h_lo[:, m_, :], t, f32(h_hi[:, m_, :]), ALU.subtract).then_inc(h_lo_ready, 1)

            def kv_body(it, first=False):
                def take(j):
                    dve.wait_ge(unit_done, LANES * it + j + 1)
                    if not first:
                        dve.wait_ge(sem(f"k_stored{j}"), 16 * it)
                        dve.wait_ge(sem("kv_turned"), LANES * it + j - 3)
                    dve.tensor_copy(tmp[:, j, 0:MEM], acc[j][:, 0:MEM]).then_inc(acc_read, 1)
                for j in range(LANES):
                    lo(*nxt(it, j))
                    if j:
                        take(j - 1)
                    if j == 1:
                        gained(0, it, tmp[:, 4, :])
                    if j == 2:
                        h_rest(0, it, tmp[:, 4, :])
                take(3)

            kv_body(0, first=True)
            loop(dve, 1, 8, kv_body)

            def norm_stats(s):
                dve.wait_ge(ss_done, s + 1)
                dve.tensor_scalar(rstd[:], mix[3][:], 1.0 / D, EPS, ALU.mult, ALU.add).then_inc(var_ready, 1)
                dve.wait_ge(std_ready, s + 1)
                dve.reciprocal(rstd[:], rstd[:]).then_inc(rstd_ready, 1)
                dve.wait_ge(rstd_ready, s + 1)

            s = n_ffn = 0
            for i, (kind, ph) in enumerate(phases):
                if kind == "ffn_in":
                    if i == 0:
                        for j in range(LANES):
                            dve.wait_ge(sem(f"k_stored{j}"), 16 * 8)
                            dve.wait_ge(sem(f"kv_stored{j}"), 16 * 8)

                    def body(it, first=False):
                        f0 = FB * n_ffn + 2 * it

                        def gate(j):
                            dve.wait_ge(unit_done, LANES * (ph.q0 + it) + j + 1)
                            dve.tensor_tensor(tmp[:, j, :], acc[j][:], rstd[:], ALU.mult).then_inc(acc_read, 1)

                        def up(j):
                            gate(j)
                            dve.wait_ge(acc_read, ph.g0 + LANES * it + j + 1)
                            dve.wait_ge(silu_done, f0 + j // 2 + 1)
                            dve.tensor_tensor(tmp[:, j, :], tmp[:, j, :], tmp[:, j - 1, :], ALU.mult).then_inc(prod_done, 1)

                        def rest(j):
                            f = 2 * it + j // 2
                            dve.wait_ge(act_hi_ready, f0 + j // 2 + 1)
                            dve.tensor_tensor(act_lo[:, f, :], tmp[:, j, :], f32(act_hi[:, f, :]),
                                              ALU.subtract).then_inc(act_lo_ready, 1)
                        lo(ph.q0 + it, 1)
                        lo(ph.q0 + it, 2)
                        if first:
                            norm_stats(s)
                        gate(0)
                        lo(ph.q0 + it, 3)
                        up(1)
                        lo(ph.q0 + it + 1, 0)
                        rest(1)
                        gate(2)
                        up(3)
                        rest(3)
                    body(0, first=True)
                    loop(dve, 1, FB // 2, body)
                elif kind == "hgrn_in":
                    att, hg = mixes[i]
                    for u in range(12):
                        lo(*nxt(ph.q0 + u // LANES, u % LANES))
                        if u == 1:
                            norm_stats(s)
                        att.vector(dve, u)
                        if u >= 8:
                            hg.vector(dve, 0, u - 8, True, False, False)

                    def body(h, finish=True):
                        for j in range(LANES):
                            lo(*nxt(ph.q0 + 2 + h, j))
                            hg.vector(dve, h, j, True, True, finish)
                    body(1, finish=False)
                    loop(dve, 2, HEADS, body)
                elif kind == "gmlp_in":
                    att, gm = mixes[i]
                    for u in range(12):
                        lo(*nxt(ph.q0 + u // LANES, u % LANES))
                        if u == 1:
                            norm_stats(s)
                        gm.setup_vector(dve, u)
                        att.vector(dve, u)
                        if u >= 8:
                            gm.v_vector(dve, 0, u - 8, first=True)

                    def v_body(it):
                        for j in range(LANES):
                            lo(*nxt(ph.q0 + 2 + it, j))
                            gm.v_vector(dve, it, j)
                            gm.v_stats(dve, it, j)
                    loop(dve, 1, 4, v_body)
                    for j in range(LANES):
                        lo(*nxt(ph.q0 + 6, j))
                        if j == 0:
                            gm.v_vector(dve, 4, 0)
                        else:
                            gm.u_vector(dve, 0, j - 1)
                        gm.v_stats(dve, 4, j)
                    gm.v_stats_end(dve)
                    gm.u_vector(dve, 0, 3)

                    def u_body(it):
                        for j in range(LANES):
                            lo(*nxt(ph.q0 + 6 + it, j))
                            gm.norm_vector(dve, it - 1, j)
                            if j:
                                gm.u_vector(dve, it, j - 1)
                                gm.mix_vector(dve, it - 1, j - 1)
                        gm.u_vector(dve, it, 3)
                        gm.mix_vector(dve, it - 1, 3)
                    u_body(1)
                    loop(dve, 2, 4, u_body)
                else:
                    rows = OUT_ROWS[kind]
                    nr = len(rows)
                    scale = 0.5 if kind == "ffn_out" else 1.0
                    s += 1
                    final = s == len(in_phases)

                    def body(it, beside=None, last=False):
                        def take(g):
                            m_, t = LANES * it + g, tmp[:, 4 + g % 2, :]
                            dve.wait_ge(unit_done, LANES * (ph.q0 + nr * it + nr - 1) + g + 1)
                            dve.scalar_tensor_tensor(x[:, m_, :], acc[g][:], scale, x[:, m_, :], ALU.mult,
                                                     ALU.add).then_inc(acc_read, 1)
                            dve.wait_ge(acc_read, ph.g0 + m_ + 1)
                            if final and m_ >= 2:
                                dve.wait_ge(sem("out_turned"), m_ - 1)
                            gained(s, m_, t)
                            if not final:
                                h_rest(s, m_, t)
                        for r in range(nr):
                            for g in range(LANES):
                                if not (last and r == nr - 1 and g == LANES - 1):
                                    lo(*nxt(ph.q0 + nr * it + r, g))
                                if beside:
                                    beside(LANES * r + g)
                                if r == nr - 1 and g:
                                    take(g - 1)
                        take(3)
                    if kind == "hgrn_out":
                        hg = mixes[i - 1][1]

                        def beside(u):
                            if u < LANES:
                                hg.vector(dve, HEADS, u, False, True, True)
                            if u == LANES:
                                hg.vector(dve, HEADS + 1, 0, False, False, True)
                        body(0, beside)
                        body(1)
                    elif kind == "gmlp_out":
                        gm = mixes[i - 1][1]

                        def beside(u):
                            if u < LANES:
                                gm.norm_vector(dve, 3, u)
                            if 1 <= u <= LANES:
                                gm.mix_vector(dve, 3, u - 1)
                        body(0, beside)
                        body(1)
                    else:
                        if final:
                            body(0)
                            body(1, last=True)
                        else:
                            loop(dve, 0, 2, body)
                        n_ffn += 1
            fin = small[:, 44:48]
            dve.wait_ge(ss_done, s + 1)
            dve.tensor_scalar(fin, acc[0][:, 0:TB], 1.0 / D, EPS, ALU.mult, ALU.add).then_inc(var_ready, 1)
            dve.wait_ge(std_ready, s + 1)
            dve.reciprocal(fin, fin).then_inc(rstd_ready, 1)
            dve.wait_ge(rstd_ready, s + 1)
            dve.wait_ge(sem("out_staged"), DB)
            for tb in (0, 2):
                dve.tensor_scalar(out_rows[:, tb, :], out_rows[:, tb, :], fin[:, tb:tb + 1], None,
                                  ALU.mult).then_inc(sem("rows_by_vector"), 1)

        @block.scalar
        def _(act):
            act.dma_start(x_raw, a["x"][0].rearrange("(tb p) c -> p tb c", p=P)).then_inc(sem("x_loaded"), 16)

            def hi(q, j, fresh=False, q_int=None):
                act.wait_ge(w_loaded[j], 16 * (q + 1))
                if not fresh:
                    act.wait_ge(unit_done, LANES * q + j - 1)
                act.activation(w_hi[:, j % 2], raw[:, j], ACT.Copy).then_inc(w_hi_ready, 1)

            act.wait_ge(sem("mem_loaded"), 16)
            for mb in range(MB):
                act.activation(mem_junk, mem_raw[:, mb, :], ACT.Square,
                               accum_out=small[:, 60 + mb:61 + mb]).then_inc(sem("mem_squared"), 1)
                act.wait_ge(sem("mem_squared"), mb + 1)
            act.wait_ge(sem("mem_var"), 1)
            act.activation(small[:, 60:62], small[:, 60:62], ACT.Sqrt).then_inc(sem("mem_std"), 1)
            hi(0, 0, fresh=True)
            act.wait_ge(sem("mem_gained"), DB)
            act.activation(mem_hi, mem_g, ACT.Copy).then_inc(sem("mem_hi_ready"), 1)
            act.wait_ge(sem("lb_shifted"), 3)
            act.activation(small[:, 72:96], small[:, 72:96], ACT.Exp).then_inc(sem("lb_exp"), 1)

            def h_top(s, m_, t):
                act.wait_ge(xg_ready, DB * s + m_ + 1)
                act.activation(h_hi[:, m_, :], t, ACT.Copy).then_inc(h_hi_ready, 1)

            def kv_body(it, first=False):
                def take(q, j, first):
                    act.wait_ge(sem("kv_turned"), LANES * q + j + 1)
                    if not first:
                        act.wait_ge(sem(f"kv_stored{j}"), 16 * q)
                    act.activation(tmp[:, j, MEM:2 * MEM], mix[j][:, 0:MEM], ACT.Copy).then_inc(sem("v_staged"), 1)
                for j in range(LANES):
                    hi(*nxt(it, j), fresh=(first and j == 0))
                    if j == 1:
                        h_top(0, it, tmp[:, 4, :])
                        if not first:
                            take(it - 1, 3, type(it) is int and it == 1)
                    if j >= 2:
                        take(it, j - 2, first)
                take(it, 2, first)

            kv_body(0, first=True)
            kv_body(1)
            loop(act, 2, 8, kv_body)
            act.wait_ge(sem("kv_turned"), 32)
            act.wait_ge(sem("kv_stored3"), 16 * 7)
            act.activation(tmp[:, 3, MEM:2 * MEM], mix[3][:, 0:MEM], ACT.Copy).then_inc(sem("v_staged"), 1)

            def root(s):
                act.wait_ge(var_ready, s + 1)
                act.activation(rstd[:], rstd[:], ACT.Sqrt).then_inc(std_ready, 1)

            s = n_ffn = 0
            for i, (kind, ph) in enumerate(phases):
                if kind == "ffn_in":
                    def body(it, first=False):
                        f0 = FB * n_ffn + 2 * it

                        def silu(j):
                            act.wait_ge(acc_read, ph.g0 + LANES * it + j + 1)
                            act.activation(tmp[:, j, :], tmp[:, j, :], ACT.Silu).then_inc(silu_done, 1)

                        def top(j):
                            act.wait_ge(prod_done, f0 + j // 2 + 1)
                            act.activation(act_hi[:, 2 * it + j // 2, :], tmp[:, j, :], ACT.Copy).then_inc(act_hi_ready, 1)
                        hi(ph.q0 + it, 1)
                        hi(ph.q0 + it, 2)
                        if first:
                            root(s)
                        silu(0)
                        hi(ph.q0 + it, 3)
                        top(1)
                        hi(ph.q0 + it + 1, 0)
                        silu(2)
                        top(3)
                    body(0, first=True)
                    loop(act, 1, FB // 2, body)
                elif kind == "hgrn_in":
                    att, hg = mixes[i]
                    for u in range(12):
                        hi(*nxt(ph.q0 + u // LANES, u % LANES))
                        if u == 1:
                            root(s)
                        att.scalar(act, u)
                        if u >= 8:
                            hg.scalar(act, 0, u - 8, True, False, False)

                    def body(h, finish=True):
                        for j in range(LANES):
                            hi(*nxt(ph.q0 + 2 + h, j))
                            hg.scalar(act, h, j, True, True, finish)
                    body(1, finish=False)
                    loop(act, 2, HEADS, body)
                elif kind == "gmlp_in":
                    att, gm = mixes[i]
                    for u in range(12):
                        hi(*nxt(ph.q0 + u // LANES, u % LANES))
                        if u == 1:
                            root(s)
                        att.scalar(act, u)
                        if u >= 8:
                            gm.v_scalar(act, 0, u - 8, first=True)

                    def v_body(it):
                        for j in range(LANES):
                            hi(*nxt(ph.q0 + 2 + it, j))
                            gm.v_scalar(act, it, j)
                    loop(act, 1, 4, v_body)
                    for j in range(LANES):
                        hi(*nxt(ph.q0 + 6, j))
                        if j == 0:
                            gm.v_scalar(act, 4, 0)
                        else:
                            if j == 1:
                                act.wait_ge(sem("v_blk_turned"), GB)
                                act.activation(work[:, GB - 1, :], mix[1][:], ACT.Copy).then_inc(sem("v_stored"), 1)
                            gm.u_scalar(act, 0, j - 1)
                    act.wait_ge(sem("v_var"), 1)
                    act.activation(gm.v_rstd, gm.v_rstd, ACT.Sqrt).then_inc(sem("v_std"), 1)
                    gm.u_scalar(act, 0, 3)

                    def u_body(it):
                        for j in range(LANES):
                            hi(*nxt(ph.q0 + 6 + it, j))
                            if j:
                                gm.u_scalar(act, it, j - 1)
                                gm.mix_scalar(act, it - 1, j - 1)
                        gm.u_scalar(act, it, 3)
                        gm.mix_scalar(act, it - 1, 3)
                    u_body(1)
                    loop(act, 2, 4, u_body)
                else:
                    nr = len(OUT_ROWS[kind])
                    s += 1
                    final = s == len(in_phases)

                    def body(it, beside=None, last=False):
                        def take(g):
                            m_, t = LANES * it + g, tmp[:, 4 + g % 2, :]
                            if not final:
                                h_top(s, m_, t)
                            else:
                                act.wait_ge(sem("out_turned"), m_ + 1)
                                act.activation(out_rows[:, :, m_ * P:(m_ + 1) * P],
                                               mix[g][:].rearrange("p (tb c) -> p tb c", tb=TB),
                                               ACT.Copy).then_inc(sem("out_staged"), 1)
                        for r in range(nr):
                            for g in range(LANES):
                                if not (last and r == nr - 1 and g == LANES - 1):
                                    hi(*nxt(ph.q0 + nr * it + r, g))
                                if beside:
                                    beside(LANES * r + g)
                                late = 2 if final else 1
                                if r == nr - 1 and g >= late:
                                    take(g - late)
                        if final:
                            take(2)
                        take(3)
                    if kind == "hgrn_out":
                        hg = mixes[i - 1][1]

                        def beside(u):
                            if u < LANES:
                                hg.scalar(act, HEADS, u, False, True, True)
                            if u == LANES:
                                hg.scalar(act, HEADS + 1, 0, False, False, True)
                        body(0, beside)
                        body(1)
                    elif kind == "gmlp_out":
                        gm = mixes[i - 1][1]
                        body(0, lambda u: gm.mix_scalar(act, 3, u - 1) if 1 <= u <= LANES else None)
                        body(1)
                    else:
                        if final:
                            body(0)
                            body(1, last=True)
                        else:
                            loop(act, 0, 2, body)
                        n_ffn += 1
            fin = small[:, 44:48]
            act.wait_ge(var_ready, s + 1)
            act.activation(fin, fin, ACT.Sqrt).then_inc(std_ready, 1)
            act.wait_ge(rstd_ready, s + 1)
            for tb in (1, 3):
                act.activation(out_rows[:, tb, :], out_rows[:, tb, :], ACT.Copy,
                               scale=fin[:, tb:tb + 1]).then_inc(sem("rows_by_scalar"), 1)

        @block.gpsimd
        def _(pool):
            pool.memset(ident[:], 0.0).then_inc(sem("consts"), 1)
            pool.memset(ones[:], 1.0).then_inc(sem("consts"), 1)
            at = 0
            for name, n in (("mem_norm", DB), ("ffn1_norm", 2 * DB), ("mix_norm", 2 * DB), ("ffn2_norm", 2 * DB),
                            ("final_norm", DB), ("lb_logits", 3 * DB), ("hgrn_gnorm", 1), ("gmlp_ln_g", GB),
                            ("gmlp_ln_b", GB)):
                v = a[name]
                flat = v if len(v.shape) == 1 else v.rearrange("l c -> (l c)")
                pool.dma_start(vec_rows[at:at + n, :], flat.rearrange("(r c) -> r c", c=P)).then_inc(sem("rows_loaded"), 16)
                at += n
            pool.wait_ge(sem("consts"), 2)
            pool.affine_select(out=ident[:], in_=ident[:], compare_op=ALU.not_equal, fill=1.0, base=0,
                               pattern=[[-1, P]], channel_multiplier=1).then_inc(sem("consts"), 1)
            pool.memset(small[:, 40:41], EPS).then_inc(sem("consts"), 1)
            mask, restart = pair[:, 0, :].bitcast(I32), pair[:, 1, :]
            pool.memset(mask, 1).then_inc(sem("masks"), 1)
            pool.memset(restart, 1.0).then_inc(sem("masks"), 1)
            pool.memset(sq_sum, 0.0).then_inc(sem("masks"), 1)
            pool.wait_ge(sem("masks"), 3)
            m4 = mask.rearrange("p (n t) -> p n t", n=TB)
            pool.affine_select(out=m4, in_=m4, compare_op=ALU.is_ge, fill=0, base=0, pattern=[[0, TB], [1, P]],
                               channel_multiplier=-1).then_inc(sem("masks"), 1)
            pool.wait_ge(sem("masks"), 4)
            late = m4[:, :, CHUNK:P]
            pool.affine_select(out=late, in_=late, compare_op=ALU.is_ge, fill=0, base=-CHUNK,
                               pattern=[[0, TB], [0, CHUNK]], channel_multiplier=1).then_inc(sem("masks"), 1)
            pool.memset(restart.rearrange("p (c t) -> p c t", t=CHUNK)[:, :, 0:1], 0.0).then_inc(sem("masks"), 1)

            def squares(s, m_, source, count):
                pool.wait_ge(source, count)
                if not (type(m_) is int and m_ == 0 and s == 0):
                    pool.wait_ge(sq_sum_ready, DB * s + m_)
                pool.tensor_tensor(sq_one, x[:, m_, :], x[:, m_, :], ALU.mult).then_inc(sq_ready, 1)
                pool.wait_ge(sq_ready, DB * s + m_ + 1)
                pool.tensor_tensor(sq_sum, sq_sum, sq_one, ALU.add).then_inc(sq_sum_ready, 1)

            def store_k(q, j):
                pool.wait_ge(acc_read, LANES * q + j + 1)
                stand_alone(pool)
                pool.dma_start(k_scratch[LANES * q + j], tmp[:, j, 0:MEM]).then_inc(sem(f"k_stored{j}"), 16)

            def store_v(q, j):
                pool.wait_ge(sem("v_staged"), LANES * q + j + 1)
                stand_alone(pool)
                pool.dma_start(v_scratch[LANES * q + j], tmp[:, j, MEM:2 * MEM]).then_inc(sem(f"kv_stored{j}"), 16)

            pool.wait_ge(sem("x_ready"), DB)

            def kv_body(it, first=False):
                for j in range(LANES):
                    if j == 0:
                        squares(0, it, sem("x_ready"), DB)
                        if not first:
                            store_v(it - 1, 3)
                    store_k(it, j)
                    if j:
                        store_v(it, j - 1)
            kv_body(0, first=True)
            loop(pool, 1, 8, kv_body)
            store_v(7, 3)

            s = 0
            for i, (kind, ph) in enumerate(phases):
                if kind == "hgrn_in":
                    att, hg = mixes[i]
                    att.load(pool)
                    pool.memset(hg.a_m, 0.0).then_inc(sem("masks"), 1)
                    for j in range(LANES):
                        hg.pool(pool, 0, j, True, False, False)

                    def body(h, finish=True):
                        for j in range(LANES):
                            hg.pool(pool, h, j, True, True, finish)
                    body(1, finish=False)
                    loop(pool, 2, HEADS, body)
                    for j in range(LANES):
                        hg.pool(pool, HEADS, j, False, True, True)
                    hg.pool(pool, HEADS + 1, 0, False, False, True)
                elif kind == "gmlp_in":
                    att, gm = mixes[i]
                    att.load(pool)
                    gm.setup_pool(pool)

                    def body(bt):
                        for j in range(LANES):
                            gm.mix_pool(pool, bt, j)
                    loop(pool, 0, 4, body)
                elif not kind.endswith("_in"):
                    s += 1
                    pool.wait_ge(ss_done, s)
                    pool.wait_ge(sem("sq_zeroed"), s - 1) if s > 1 else None
                    if kind == "gmlp_out":
                        pool.wait_ge(sem("mix_lo"), GB)
                    pool.memset(sq_sum, 0.0).then_inc(sem("sq_zeroed"), 1)
                    pool.wait_ge(sem("sq_zeroed"), s)

                    def body(it):
                        for g in range(LANES):
                            m_ = LANES * it + g
                            squares(s, m_, acc_read, ph.g0 + m_ + 1)
                    loop(pool, 0, 2, body)


_INS = ["x", "mem", "mem_norm", "lb_logits", "ffn1_norm", "ffn1_w_in", "ffn1_w_out", "mix_norm", "mem_w_kv",
        "hgrn_w_in", "hgrn_gnorm", "hgrn_w_out", "gmlp_w_in", "gmlp_ln_g", "gmlp_ln_b", "gmlp_w_s", "gmlp_b_s",
        "gmlp_w_out", "ffn2_norm", "ffn2_w_in", "ffn2_w_out", "final_norm"]
_OUTS = [((1, T, D), "float32")]


def kernel(**inputs):
    import concourse.bacc as _bacc
    from concourse.bass_utils import run_bass_kernel_spmd as _run

    nc = _bacc.Bacc("TRN2", target_bir_lowering=False, num_devices=1)
    arrays, args = {}, {}
    for name in _INS:
        arr = np.ascontiguousarray(inputs[name])
        arrays[f"in_{name}_dram"] = arr
        args[name] = nc.dram_tensor(f"in_{name}_dram", arr.shape, mybir.dt.from_np(arr.dtype),
                                    kind="ExternalInput").ap()
    outs = []
    for i, (shape, dtype) in enumerate(_OUTS):
        dt = mybir.dt.from_np(np.dtype(dtype))
        outs.append(nc.dram_tensor(f"out_{i}_dram", shape, dt, kind="ExternalOutput").ap())
    hybrid_trunk(nc, args, outs[0])
    r = _run(nc, [arrays], core_ids=[0])
    return r.results[0]["out_0_dram"]
```

```python
from contextlib import ExitStack

import numpy as np

import concourse.bass as bass
from concourse import mybir
from concourse.alu_op_type import AluOpType as ALU

F32 = mybir.dt.float32
F32R = mybir.dt.float32r
I32 = mybir.dt.int32
ACT = mybir.ActivationFunctionType
AX_X = mybir.AxisListType.X

P = 128
EPS = 1e-6
D = 1024
DB = D // P
T = 512
MEM = 256
MB = MEM // P
FF = 2816
FB = FF // P
HEADS = 8
CHUNK = 64
NCH = T // CHUNK
TB = T // P
GW = 2048
GB = GW // P
GROUPS = 8
XH = 4
XSCALE = 256 ** -0.5
KU = 8
LANES = 4

VECTORS = (("mem_norm", DB), ("ffn1_norm", 2 * DB), ("mix_norm", 2 * DB), ("ffn2_norm", 2 * DB),
           ("final_norm", DB), ("lb_logits", 3 * DB), ("hgrn_gnorm", 1), ("gmlp_ln_g", GB), ("gmlp_ln_b", GB))
ROWS = {}
_at = 0
for _name, _n in VECTORS:
    ROWS[_name] = _at
    _at += _n
NROWS = _at
assert NROWS <= P


class Phase:

    quad = 0
    group = 0

    def __init__(self, units, groups):
        self.q0, self.g0 = Phase.quad, Phase.group
        self.units, self.groups = units, groups
        Phase.quad += units // LANES
        Phase.group += groups

    @property
    def end_quad(self):
        return self.q0 + self.units // LANES


def hybrid_trunk(nc, a, out):
    Phase.quad = Phase.group = 0
    kv = Phase(32, 32)
    phases = []
    for kind, units, groups in (("ffn_in", 44, 44), ("ffn_out", 24, 8), ("hgrn_in", 40, 40), ("hgrn_out", 16, 8),
                                ("ffn_in", 44, 44), ("ffn_out", 24, 8), ("ffn_in", 44, 44), ("ffn_out", 24, 8),
                                ("gmlp_in", 40, 40), ("gmlp_out", 24, 8), ("ffn_in", 44, 44), ("ffn_out", 24, 8)):
        phases.append((kind, Phase(units, groups)))
    LAST_QUAD = Phase.quad

    def blocks_of(w):
        return w.rearrange("(kb p) c -> p kb c", p=P)

    ffn_w = [(blocks_of(a[f"{n}_w_in"][i]), blocks_of(a[f"{n}_w_out"][i]))
             for i, n in ((0, "ffn1"), (0, "ffn2"), (1, "ffn1"), (1, "ffn2"))]
    hgrn_w = blocks_of(a["hgrn_w_in"][0]), blocks_of(a["hgrn_w_out"][0])
    gmlp_w = blocks_of(a["gmlp_w_in"][0]), blocks_of(a["gmlp_w_out"][0])
    kv_w = [blocks_of(a["mem_w_kv"][i]) for i in range(2)]
    OUT_ROWS = {"ffn_out": [(0, 0, 8), (8, 8, 8), (16, 16, FB - 16)],
                "hgrn_out": [(8, 16, 8), (0, 0, 8)],
                "gmlp_out": [(16, 16, 8), (0, 0, 8), (8, 8, 8)]}
    GAINS = [ROWS["ffn1_norm"], ROWS["mix_norm"], ROWS["ffn2_norm"],
             ROWS["ffn1_norm"] + DB, ROWS["mix_norm"] + DB, ROWS["ffn2_norm"] + DB, ROWS["final_norm"]]

    k_scratch = nc.dram_tensor("k_scratch", (32, P, MEM), F32).ap()
    v_scratch = nc.dram_tensor("v_scratch", (32, P, MEM), F32).ap()

    with ExitStack() as ctx:
        def sb(name, shape, dt=F32):
            return ctx.enter_context(nc.sbuf_tensor(name, shape, dt))

        sems = {}

        def sem(name):
            if name not in sems:
                sems[name] = ctx.enter_context(nc.semaphore(name))
            return sems[name]

        x = sb("x", [P, DB, T])
        with nc.sbuf_tensor("raw", [P, LANES, KU, P], F32) as raw:
            pass
        w_lo = sb("w_lo", [P, LANES, KU, P], F32R)
        w_hi = sb("w_hi", [P, LANES, KU, P], F32R)
        ident = sb("ident", [P, P])
        ones = sb("ones", [P, P])
        vecs = sb("vecs", [P, NROWS])
        rstd = sb("rstd", [P, T])
        sq = sb("sq", [P, 2, T])
        tmp = sb("tmp", [P, 6, T])
        pair = sb("pair", [P, 2, T])
        bs_all = sb("bs_all", [P, GROUPS, P])
        q_row = sb("q_row", [P, P])
        small = sb("small", [P, 96])
        with nc.sbuf_tensor("h_hi", [P, DB, T], F32R) as h_hi, nc.sbuf_tensor("h_lo", [P, DB, T], F32R) as h_lo:
            pass
        out_rows = sb("out_rows", [P, 2 * DB, T])[:, 0:DB, :].rearrange("p b t -> p (b t)").rearrange(
            "p (tb c) -> p tb c", tb=TB)
        with nc.sbuf_tensor("act_hi", [P, 24, T], F32R) as act_hi, nc.sbuf_tensor("act_lo", [P, 24, T], F32R) as act_lo:
            pass
        work = sb("work", [P, 48, T])

        acc = [ctx.enter_context(nc.psum_tensor(f"acc{i}", [P, T], F32)) for i in range(LANES)]
        mix = [ctx.enter_context(nc.psum_tensor(f"mix{i}", [P, T], F32)) for i in range(4)]

        sq_sum, sq_one = sq[:, 0, :], sq[:, 1, :]
        mem_hi = act_hi[:, 0:4, :].rearrange("p b (k m) -> p (b k) m", k=2)
        mem_lo = act_lo[:, 0:4, :].rearrange("p b (k m) -> p (b k) m", k=2)
        mem_raw = work[:, 40:44, :].rearrange("p b t -> p (b t)").rearrange("p (mb c) -> p mb c", mb=MB)
        mem_g = work[:, 44:48, :].rearrange("p b (k m) -> p (b k) m", k=2)
        mem_junk = work[:, 36:38, :].rearrange("p b t -> p (b t)")
        x_raw = work[:, 16:24, :].rearrange("p b t -> p (b t)").rearrange("p (tb c) -> p tb c", tb=TB)
        vec_rows = work[:, 38, 0:P]

        def f32(ap):
            return ap.bitcast(F32)

        def loop(eng, lo, hi, body):
            if hi - lo == 1:
                body(lo)
            else:
                with eng.Fori(lo, hi) as it:
                    body(it)

        def stand_alone(eng):
            eng.sem_inc(sem("wait_passed"), 1)

        def ahead(q, j):
            return (q, j + 2) if j + 2 < LANES else (q + 1, j - 2)

        def blocks_ahead(kind, r, g):
            rows = OUT_ROWS[kind]
            return rows[(r + (g >= 2)) % len(rows)][2]

        w_loaded = [sem(f"w_loaded{j}") for j in range(LANES)]
        w_hi_ready, w_lo_ready = sem("w_hi_ready"), sem("w_lo_ready")
        unit_done = sem("unit_done")
        acc_read = sem("acc_read")
        xg_ready, h_hi_ready, h_lo_ready = sem("xg_ready"), sem("h_hi_ready"), sem("h_lo_ready")
        sq_ready, sq_sum_ready = sem("sq_ready"), sem("sq_sum_ready")
        ss_done, var_ready, std_ready, rstd_ready = (sem("ss_done"), sem("var_ready"), sem("std_ready"),
                                                     sem("rstd_ready"))
        silu_done, prod_done, act_hi_ready, act_lo_ready = (sem("silu_done"), sem("prod_done"), sem("act_hi_ready"),
                                                            sem("act_lo_ready"))

        class Attention:
            def __init__(self, layer, phase, kv_at, tmp_at):
                self.layer, self.ph = layer, phase
                self.kT = work[:, kv_at:kv_at + 4, :].rearrange("p b (k m) -> p (b k) m", k=2)
                self.v = work[:, kv_at + 4:kv_at + 8, :].rearrange("p b (k mb c) -> p (b k) mb c", k=2, mb=MB)
                self.qT = work[:, tmp_at:tmp_at + 4, :]
                self.p = work[:, tmp_at + 4:tmp_at + 6, :].rearrange("p b (k m) -> p (b k) m", k=2)
                self.pT = work[:, tmp_at + 6:tmp_at + 8, :]

            def load(self, pool):
                pool.wait_ge(unit_done, LANES * self.ph.q0)
                for j in range(LANES):
                    pool.wait_ge(sem(f"k_stored{j}"), 16 * 8)
                    pool.wait_ge(sem(f"kv_stored{j}"), 16 * 8)
                b = 16 * self.layer
                pool.dma_start(self.kT, k_scratch[b:b + DB].rearrange("b p m -> p b m")).then_inc(sem("kv_loaded"), 16)
                pool.dma_start(self.v.rearrange("p b mb c -> p b (mb c)"),
                               v_scratch[b + DB:b + 2 * DB].rearrange("b p m -> p b m")).then_inc(sem("kv_loaded"), 16)

            def tensor(self, pe, s):
                if s % 2 == 0 and 0 <= (s - 4) // 2 < XH and s >= 4:
                    h = (s - 4) // 2
                    n = XH * self.layer + h
                    pe.wait_ge(sem("pT_ready"), 2 * (n + 1))
                    for dv in range(2):
                        for mb in range(MB):
                            m = pe.matmul(mix[2 + dv][:], self.v[:, 2 * h + dv, mb, :], self.pT[:, mb, :],
                                          start=(mb == 0), stop=(mb == MB - 1))
                    m.then_inc(sem("pv_done"), 1)
                if s % 2 == 0 and s >= 2 and (s - 2) // 2 < XH:
                    h = (s - 2) // 2
                    n = XH * self.layer + h
                    if h == 0:
                        pe.wait_ge(sem("kv_loaded"), 32 * (self.layer + 1))
                    pe.wait_ge(acc_read, self.ph.g0 + 2 * h + 2)
                    if n:
                        pe.wait_ge(sem("exp_done"), TB * n)
                    for tb in range(TB):
                        for d in range(2):
                            m = pe.matmul(mix[tb // 2][:, (tb % 2) * MEM:(tb % 2 + 1) * MEM],
                                          self.qT[:, 2 * (h % 2) + d, tb * P:(tb + 1) * P],
                                          self.kT[:, 2 * h + d, :], start=(d == 0), stop=(d == 1))
                    m.then_inc(sem("scores_done"), 1)
                if s % 2 == 1 and s >= 3 and (s - 3) // 2 < XH:
                    h = (s - 3) // 2
                    n = XH * self.layer + h
                    pe.wait_ge(sem("p_ready"), TB * (n + 1))
                    if n:
                        pe.wait_ge(sem("o_mem_lo"), 2 * n)
                    for mb in range(MB):
                        for tb in range(TB):
                            m = pe.transpose(mix[2 + mb][:, tb * P:(tb + 1) * P],
                                             self.p[:, tb, mb * P:(mb + 1) * P], ident[:])
                    m.then_inc(sem("p_turned"), 1)

            def vector(self, dve, s):
                if 1 <= s <= 2 * XH:
                    u = s - 1
                    dve.wait_ge(unit_done, LANES * self.ph.q0 + u + 1)
                    if u >= 4:
                        dve.wait_ge(sem("scores_done"), XH * self.layer + u // 2 - 1)
                    dve.tensor_tensor(self.qT[:, u % 4, :], acc[u % LANES][:], rstd[:], ALU.mult).then_inc(acc_read, 1)
                if s % 2 == 1 and s >= 3 and (s - 3) // 2 < XH:
                    n = XH * self.layer + (s - 3) // 2
                    mx, neg, tot, inv = small[:, 0:4], small[:, 4:8], small[:, 8:12], small[:, 12:16]
                    dve.wait_ge(sem("scores_done"), n + 1)
                    for b in range(2):
                        dve.tensor_reduce(mx[:, 2 * b:2 * b + 2], mix[b][:].rearrange("p (k m) -> p k m", k=2), AX_X,
                                          ALU.max).then_inc(sem("max_done"), 1)
                    dve.wait_ge(sem("max_done"), 2 * (n + 1))
                    dve.tensor_scalar(neg, mx, -XSCALE, None, ALU.mult).then_inc(sem("neg_max_ready"), 1)
                if s % 2 == 1 and s >= 5 and (s - 5) // 2 < XH:
                    h = (s - 5) // 2
                    n = XH * self.layer + h
                    for dv in range(2):
                        b = 16 + 2 * h + dv
                        dve.wait_ge(sem("o_mem_hi"), 2 * n + dv + 1)
                        dve.tensor_tensor(act_lo[:, b, :], mix[2 + dv][:], f32(act_hi[:, b, :]),
                                          ALU.subtract).then_inc(sem("o_mem_lo"), 1)
                if s % 2 == 1 and s >= 3 and (s - 3) // 2 < XH:
                    n = XH * self.layer + (s - 3) // 2
                    dve.wait_ge(sem("exp_done"), TB * (n + 1))
                    dve.reciprocal(inv, tot).then_inc(sem("inv_ready"), 1)
                    dve.wait_ge(sem("inv_ready"), n + 1)
                    for tb in range(TB):
                        dve.tensor_scalar(self.p[:, tb, :], self.p[:, tb, :], inv[:, tb:tb + 1], None,
                                          ALU.mult).then_inc(sem("p_ready"), 1)

            def scalar(self, act, s):
                if s % 2 == 1 and s >= 5 and (s - 5) // 2 < XH:
                    h = (s - 5) // 2
                    n = XH * self.layer + h
                    act.wait_ge(sem("pv_done"), n + 1)
                    for dv in range(2):
                        act.activation(act_hi[:, 16 + 2 * h + dv, :], mix[2 + dv][:],
                                       ACT.Copy).then_inc(sem("o_mem_hi"), 1)
                if s % 2 == 1 and s >= 3 and (s - 3) // 2 < XH:
                    h = (s - 3) // 2
                    n = XH * self.layer + h
                    act.wait_ge(sem("neg_max_ready"), n + 1)
                    if n:
                        act.wait_ge(sem("p_turned"), n)
                    for tb in range(TB):
                        act.activation(self.p[:, tb, :], mix[tb // 2][:, (tb % 2) * MEM:(tb % 2 + 1) * MEM], ACT.Exp,
                                       bias=small[:, 4 + tb:5 + tb], scale=XSCALE,
                                       accum_out=small[:, 8 + tb:9 + tb]).then_inc(sem("exp_done"), 1)
                if s % 2 == 0 and s >= 4 and (s - 4) // 2 < XH:
                    h = (s - 4) // 2
                    n = XH * self.layer + h
                    act.wait_ge(sem("p_turned"), n + 1)
                    if n:
                        act.wait_ge(sem("pv_done"), n)
                    for mb in range(MB):
                        act.activation(self.pT[:, mb, :], mix[2 + mb][:], ACT.Copy).then_inc(sem("pT_ready"), 1)

        class Hgrn:
            def __init__(self, phase):
                self.ph = phase
                (self.q, self.k, self.b, self.eb, self.enb, self.qdec, self.kinv,
                 self.khat) = (work[:, 8 + i, :] for i in range(8))
                self.vT, self.sg, self.khat_t, self.v_t, self.a_m = (work[:, 32 + i, :] for i in range(5))
                self.state = work[:, 37:39, :].rearrange("p b t -> p (b t)")
                self.mask = pair[:, 0, :].bitcast(I32)
                self.restart = pair[:, 1, :]
                self.decay = small[:, 16:16 + NCH]
                self.lb = small[:, 24:32]
                self.one_less_lb = small[:, 32:40]

            def tensor(self, pe, h, j, finish):
                n = h - 1
                pairs = [slice(P * i, P * (i + 1)) for i in range(TB)]
                if j == 0:
                    if finish:
                        pe.wait_ge(sem("state_done"), (NCH - 1) * n)
                    else:
                        pe.wait_ge(sem("o_mem_lo"), 2 * XH)
                    pe.wait_ge(acc_read, self.ph.g0 + 2 * XH + LANES * h - 1)
                    for c in pairs:
                        m = pe.transpose(mix[3][:, c], self.vT[:, c], ident[:])
                    m.then_inc(sem("v_turned"), 1)
                    pe.wait_ge(sem("qdec_ready"), 2 * (n + 1))
                    if finish:
                        pe.wait_ge(sem("o_log"), n)
                    for i, c in enumerate(pairs):
                        m = pe.matmul(mix[2][:, c], self.kinv[:, c], self.qdec[:, c], start=True, stop=True)
                    m.then_inc(sem("a_done"), 1)
                    pe.wait_ge(sem("khat_ready"), n + 1)
                    for c in pairs:
                        m = pe.transpose(mix[0][:, c], self.khat[:, c], ident[:])
                    m.then_inc(sem("khat_turned"), 1)
                if j == 1:
                    pe.wait_ge(sem("khat_t_ready"), n + 1)
                    pe.wait_ge(sem("v_t_ready"), n + 1)
                    for c in range(NCH - 1):
                        half, cols = slice(CHUNK * (c % 2), CHUNK * (c % 2 + 1)), pairs[c // 2]
                        bank = mix[3 * (c % 2)]
                        m = pe.matmul(bank[:, P * (c // 2):P * (c // 2 + 1)], self.khat_t[half, cols],
                                      self.v_t[half, cols], start=True, stop=True)
                    m.then_inc(sem("kv_done"), 1)
                    pe.wait_ge(sem("a_masked"), n + 1)
                    if finish:
                        pe.wait_ge(sem("o_scaled"), n)
                    for i, c in enumerate(pairs):
                        pe.matmul(mix[1][:, c], self.v_t[:, c], self.a_m[:, c], start=(i == 0), stop=False,
                                  skip_group_check=True)
                if j == 2:
                    pe.wait_ge(sem("state_done"), (NCH - 1) * (n + 1))
                    for c in range(1, NCH):
                        cols = slice(CHUNK * c, CHUNK * (c + 1))
                        m = pe.matmul(mix[1][:, cols], self.state[:, P * (c - 1):P * c], self.qdec[:, cols],
                                      start=False, stop=(c == NCH - 1), skip_group_check=True)
                    m.then_inc(sem("o_done"), 1)
                if j == 3:
                    pe.wait_ge(sem("o_squared"), n + 1)
                    pe.matmul(mix[2][:], ones[:], tmp[:, 4, :], start=True, stop=True).then_inc(sem("oss_done"), 1)

            def unit_of(self, h, j):
                return LANES * (self.ph.q0 + 2 + h) + j

            def vector(self, dve, h, j, own, mixer, finish):
                n = h - 1
                if j == 0:
                    if mixer:
                        dve.wait_ge(sem("khat_ready"), n + 1)
                        dve.wait_ge(unit_done, self.unit_of(h, 0))
                        dve.tensor_tensor(tmp[:, 2, :], acc[3][:], rstd[:], ALU.mult).then_inc(acc_read, 1)
                    if finish:
                        dve.wait_ge(sem("o_rstd"), n)
                        dve.scalar_tensor_tensor(tmp[:, 5, :], mix[1][:], vecs[:, ROWS["hgrn_gnorm"]:ROWS["hgrn_gnorm"] + 1],
                                                 tmp[:, 5, :], ALU.mult, ALU.mult).then_inc(sem("o_scaled"), 1)
                    if own:
                        if mixer:
                            dve.wait_ge(sem("q_ready"), n + 1)
                        dve.wait_ge(unit_done, self.unit_of(h, 1))
                        dve.tensor_tensor(tmp[:, 0, :], acc[0][:], rstd[:], ALU.mult).then_inc(acc_read, 1)
                    if mixer:
                        dve.wait_ge(sem("g_den"), n + 1)
                        dve.reciprocal(tmp[:, 3, :], tmp[:, 3, :]).then_inc(sem("g_sig"), 1)
                        dve.wait_ge(sem("a_done"), n + 1)
                        stand_alone(dve)
                        dve.copy_predicated(self.a_m, self.mask, mix[2][:]).then_inc(sem("a_masked"), 1)
                    if finish:
                        dve.wait_ge(sem("o_hi"), n)
                        dve.tensor_tensor(act_lo[:, h - 2, :], tmp[:, 4, :], f32(act_hi[:, h - 2, :]),
                                          ALU.subtract).then_inc(sem("o_lo"), 1)
                if j == 2:
                    if own:
                        dve.wait_ge(unit_done, self.unit_of(h, 2))
                        if mixer:
                            dve.wait_ge(sem("g_ready"), n + 1)
                        dve.tensor_tensor(tmp[:, 2, :], acc[1][:], rstd[:], ALU.mult).then_inc(acc_read, 1)
                    if mixer:
                        dve.wait_ge(sem("kv_done"), n + 1)
                        for c in range(NCH - 1):
                            dst = self.state[:, P * c:P * (c + 1)]
                            kv_c = mix[3 * (c % 2)][:, P * (c // 2):P * (c // 2 + 1)]
                            if c == 0:
                                dve.tensor_copy(dst, kv_c).then_inc(sem("state_done"), 1)
                            else:
                                dve.wait_ge(sem("state_done"), (NCH - 1) * n + c)
                                dve.scalar_tensor_tensor(dst, self.state[:, P * (c - 1):P * c], self.decay[:, c:c + 1],
                                                         kv_c, ALU.mult, ALU.add).then_inc(sem("state_done"), 1)
                    if own:
                        lb, one_less = bass.ds(24 + h, 1), bass.ds(32 + h, 1)
                        dve.wait_ge(sem("f_den"), h + 1)
                        dve.reciprocal(tmp[:, 3, :], tmp[:, 3, :]).then_inc(sem("f_sig"), 1)
                        dve.wait_ge(sem("f_sig"), h + 1)
                        dve.tensor_scalar(tmp[:, 3, :], tmp[:, 3, :], small[:, one_less], small[:, lb], ALU.mult,
                                          ALU.add).then_inc(sem("f_ready"), 1)
                if j == 3 and own:
                    dve.wait_ge(unit_done, self.unit_of(h, 3))
                    dve.tensor_tensor(self.vT, acc[2][:], rstd[:], ALU.mult).then_inc(acc_read, 1)
                    dve.wait_ge(sem("logf_ready"), h + 1)
                    dve.tensor_tensor_scan(self.b, self.restart, tmp[:, 2, :], 0.0, ALU.mult,
                                           ALU.add).then_inc(sem("b_ready"), 1)
                    dve.wait_ge(sem("b_ready"), h + 1)
                    b3 = self.b.rearrange("p (c t) -> p c t", t=CHUNK)
                    dve.tensor_tensor(tmp[:, 2, :].rearrange("p (c t) -> p c t", t=CHUNK),
                                      b3[:, :, CHUNK - 1:CHUNK].to_broadcast([P, NCH, CHUNK]), b3,
                                      ALU.subtract).then_inc(sem("rest_ready"), 1)
                    dve.wait_ge(sem("eb_ready"), h + 1)
                    dve.tensor_copy(self.decay.rearrange("p (c o) -> p c o", o=1),
                                    self.eb.rearrange("p (c t) -> p c t",
                                                      t=CHUNK)[:, :, CHUNK - 1:CHUNK]).then_inc(sem("decay_ready"), 1)
                    dve.wait_ge(sem("q_den"), h + 1)
                    dve.reciprocal(tmp[:, 1, :], tmp[:, 1, :]).then_inc(sem("q_sig"), 1)

            def scalar(self, act, h, j, own, mixer, finish):
                n = h - 1
                g_at = self.ph.g0 + 2 * XH + LANES * h
                if j == 0:
                    if finish:
                        act.wait_ge(sem("oss_done"), n)
                        act.activation(tmp[:, 5, :], mix[2][:], ACT.Ln, bias=small[:, 40:41],
                                       scale=1.0 / P).then_inc(sem("o_log"), 1)
                        act.wait_ge(sem("o_log"), n)
                        act.activation(tmp[:, 5, :], tmp[:, 5, :], ACT.Exp, scale=-0.5).then_inc(sem("o_rstd"), 1)
                    if mixer:
                        act.wait_ge(acc_read, g_at)
                        act.activation(tmp[:, 3, :], tmp[:, 2, :], ACT.Exp, scale=-1.0).then_inc(sem("g_exp"), 1)
                        act.wait_ge(sem("g_exp"), n + 1)
                        act.activation(tmp[:, 3, :], tmp[:, 3, :], ACT.Identity, bias=ones[:, 0:1]).then_inc(sem("g_den"), 1)
                    if own:
                        act.wait_ge(acc_read, g_at + 1)
                        act.activation(tmp[:, 1, :], tmp[:, 0, :], ACT.Exp, scale=-1.0).then_inc(sem("q_exp"), 1)
                        act.wait_ge(sem("q_exp"), h + 1)
                        act.activation(tmp[:, 1, :], tmp[:, 1, :], ACT.Identity, bias=ones[:, 0:1]).then_inc(sem("q_den"), 1)
                    if mixer:
                        act.wait_ge(sem("v_turned"), n + 1)
                        act.activation(self.v_t, mix[3][:], ACT.Copy).then_inc(sem("v_t_ready"), 1)
                        act.wait_ge(sem("khat_turned"), n + 1)
                        act.activation(self.khat_t, mix[0][:], ACT.Copy).then_inc(sem("khat_t_ready"), 1)
                    if finish:
                        act.wait_ge(sem("o_gated"), n)
                        act.activation(act_hi[:, h - 2, :], tmp[:, 4, :], ACT.Copy).then_inc(sem("o_hi"), 1)
                if j == 2 and own:
                    act.wait_ge(acc_read, g_at + 2)
                    act.activation(tmp[:, 3, :], tmp[:, 2, :], ACT.Exp, scale=-1.0).then_inc(sem("f_exp"), 1)
                    act.wait_ge(sem("f_exp"), h + 1)
                    act.activation(tmp[:, 3, :], tmp[:, 3, :], ACT.Identity, bias=ones[:, 0:1]).then_inc(sem("f_den"), 1)
                    act.wait_ge(sem("f_ready"), h + 1)
                    act.activation(tmp[:, 2, :], tmp[:, 3, :], ACT.Ln).then_inc(sem("logf_ready"), 1)
                if j == 3:
                    if mixer:
                        act.wait_ge(sem("o_done"), n + 1)
                        if finish:
                            act.wait_ge(sem("o_lo"), n)
                        act.activation(tmp[:, 4, :], mix[1][:], ACT.Square).then_inc(sem("o_squared"), 1)
                    if own:
                        act.wait_ge(sem("b_ready"), h + 1)
                        act.activation(self.eb, self.b, ACT.Exp).then_inc(sem("eb_ready"), 1)
                        act.activation(self.enb, self.b, ACT.Exp, scale=-1.0).then_inc(sem("enb_ready"), 1)
                        act.wait_ge(sem("rest_ready"), h + 1)
                        act.activation(tmp[:, 2, :], tmp[:, 2, :], ACT.Exp).then_inc(sem("rest_exp"), 1)

            def pool(self, pool, h, j, own, mixer, finish):
                n = h - 1
                if j == 0:
                    if finish:
                        pool.wait_ge(sem("g_ready"), n)
                        pool.wait_ge(sem("o_scaled"), n)
                        pool.tensor_tensor(tmp[:, 4, :], tmp[:, 5, :], self.sg, ALU.mult).then_inc(sem("o_gated"), 1)
                    if mixer:
                        pool.wait_ge(sem("g_sig"), n + 1)
                        if finish:
                            pool.wait_ge(sem("o_gated"), n)
                        pool.tensor_tensor(self.sg, tmp[:, 2, :], tmp[:, 3, :], ALU.mult).then_inc(sem("g_ready"), 1)
                if j == 2 and own:
                    pool.wait_ge(sem("f_ready"), h + 1)
                    stand_alone(pool)
                    pool.tensor_scalar(self.k, tmp[:, 3, :], -1.0, 1.0, ALU.mult, ALU.add).then_inc(sem("k_ready"), 1)
                if j == 3 and own:
                    if mixer:
                        pool.wait_ge(sem("o_done"), n + 1)
                    pool.wait_ge(sem("k_ready"), h + 1)
                    pool.wait_ge(sem("enb_ready"), h + 1)
                    pool.tensor_tensor(self.kinv, self.k, self.enb, ALU.mult).then_inc(sem("qdec_ready"), 1)
                    pool.wait_ge(sem("rest_exp"), h + 1)
                    pool.tensor_tensor(self.khat, self.k, tmp[:, 2, :], ALU.mult).then_inc(sem("khat_ready"), 1)
                    pool.wait_ge(sem("q_sig"), h + 1)
                    pool.tensor_tensor(self.q, tmp[:, 0, :], tmp[:, 1, :], ALU.mult).then_inc(sem("q_ready"), 1)
                    pool.wait_ge(sem("q_ready"), h + 1)
                    pool.tensor_tensor(self.qdec, self.q, self.eb, ALU.mult).then_inc(sem("qdec_ready"), 1)

        class Gmlp:
            def __init__(self, phase):
                self.ph = phase
                self.w_raw = pair[:].rearrange("p b (k s) -> p (b k) s", s=P)
                self.w_turned = pair[:].rearrange("p b (k s) -> p (b k) s", s=P)
                self.row_sums = sq[:].rearrange("p b (k s) -> p (b k) s", s=P)
                self.mean_var = small[:, 48:56].rearrange("p (n z) -> p n z", z=2)
                self.v_rstd = small[:, 56:60]

            def setup_pool(self, pool):
                pool.wait_ge(sem("o_lo"), HEADS)
                pool.wait_ge(sem("b_ready"), HEADS)
                pool.dma_start(self.w_raw, a["gmlp_w_s"][0].rearrange("g t s -> t g s")).then_inc(sem("ws_loaded"), 16)
                pool.dma_start(bs_all[:], a["gmlp_b_s"][0:1].to_broadcast([P, GROUPS, P])).then_inc(sem("bs_loaded"), 16)
                pool.wait_ge(sem("ws_loaded"), 16)
                pool.affine_select(out=self.w_raw, in_=self.w_raw, compare_op=ALU.is_ge, fill=0.0, base=0,
                                   pattern=[[0, GROUPS], [-1, P]], channel_multiplier=1).then_inc(sem("ws_masked"), 1)

            def setup_tensor(self, pe, s):
                if s == 1:
                    pe.wait_ge(sem("ws_masked"), 1)
                    for g in range(GROUPS):
                        m = pe.transpose(mix[g // 4][:, P * (g % 4):P * (g % 4 + 1)], self.w_raw[:, g, :], ident[:])
                    m.then_inc(sem("ws_turned"), 1)
                if s == 2:
                    pe.wait_ge(sem("wt_ready"), 2)
                    for b in range(2):
                        m = pe.matmul(mix[2 + b][:], ones[:], pair[:, b, :], start=True, stop=True)
                    m.then_inc(sem("row_sums_done"), 1)
                if s == 3:
                    pe.wait_ge(sem("row_sums_ready"), 2)

            def setup_vector(self, dve, s):
                if s == 2:
                    dve.wait_ge(sem("ws_turned"), 1)
                    for b in range(2):
                        dve.tensor_copy(pair[:, b, :], mix[b][:]).then_inc(sem("wt_ready"), 1)
                if s == 3:
                    dve.wait_ge(sem("row_sums_done"), 1)
                    for b in range(2):
                        dve.tensor_copy(sq[:, b, :], mix[2 + b][:]).then_inc(sem("row_sums_ready"), 1)

            def v_tensor(self, pe, it, j, first=False):
                if first and j == 0:
                    return
                c = LANES * it + j
                b = (j - 1) % 2
                pe.wait_ge(sem("v_gelu"), c)
                if not first or j == 3:
                    pe.wait_ge(sem("v_stored"), c - 2)
                for n in range(TB):
                    m = pe.transpose(mix[b][:, P * n:P * (n + 1)], tmp[:, b, P * n:P * (n + 1)], ident[:])
                m.then_inc(sem("v_blk_turned"), 1)

            def v_vector(self, dve, it, j, first=False):
                c = LANES * it + j
                if not (first and j == 0):
                    b = (j - 1) % 2
                    dve.wait_ge(unit_done, LANES * (self.ph.q0 + 2) + c)
                    if not first or j == 3:
                        dve.wait_ge(sem("v_blk_turned"), c - 2)
                    dve.tensor_tensor(tmp[:, b, :], acc[(j - 1) % LANES][:], rstd[:], ALU.mult).then_inc(acc_read, 1)

            def v_stats(self, dve, it, j):
                if j >= 2:
                    dve.wait_ge(sem("v_stored"), LANES * it)
                    for n in (2 * j - 4, 2 * j - 3):
                        dve.bn_stats(v_stats_sb[:, n, it - 1, :], work[:, bass.ds(LANES * (it - 1), LANES), P * n:P * (n + 1)]
                                     ).then_inc(sem("v_stats"), 1)

            def v_stats_end(self, dve):
                dve.wait_ge(sem("v_stats"), 4 * TB)
                for n in range(TB):
                    dve.bn_aggr(self.mean_var[:, n, :], v_stats_sb[:, n, :, :]).then_inc(sem("v_aggr"), 1)
                dve.wait_ge(sem("v_aggr"), TB)
                dve.tensor_scalar(self.v_rstd.rearrange("p (n z) -> p n z", z=1), self.mean_var[:, :, 1:2], EPS, None,
                                  ALU.add).then_inc(sem("v_var"), 1)
                dve.wait_ge(sem("v_std"), 1)
                dve.reciprocal(self.v_rstd, self.v_rstd).then_inc(sem("v_rstd"), 1)

            def v_scalar(self, act, it, j, first=False):
                c = LANES * it + j
                if not (first and j < 2):
                    act.wait_ge(sem("v_blk_turned"), c - 1)
                    act.activation(work[:, c - 2, :], mix[(j - 2) % 2][:], ACT.Copy).then_inc(sem("v_stored"), 1)
                if not (first and j < 1):
                    act.wait_ge(acc_read, self.ph.g0 + 2 * XH + c)
                    b = (j - 1) % 2
                    act.activation(tmp[:, b, :], tmp[:, b, :], ACT.Gelu).then_inc(sem("v_gelu"), 1)

            def u_vector(self, dve, it, j):
                c = LANES * it + j
                dve.wait_ge(unit_done, LANES * (self.ph.q0 + 6) + c + 1)
                if type(it) is not int or c >= 2:
                    dve.wait_ge(sem("u_ready"), c - 1)
                else:
                    dve.wait_ge(sem("v_blk_turned"), GB)
                dve.tensor_tensor(tmp[:, j % 2, :], acc[j][:], rstd[:], ALU.mult).then_inc(acc_read, 1)

            def u_scalar(self, act, it, j):
                c = LANES * it + j
                act.wait_ge(acc_read, self.ph.g0 + 2 * XH + GB + c + 1)
                act.activation(work[:, 24 + c, :], tmp[:, j % 2, :], ACT.Gelu).then_inc(sem("u_ready"), 1)

            def norm_vector(self, dve, bt, j):
                m = LANES * bt + j
                if type(bt) is not int or m >= 2:
                    dve.wait_ge(sem("mixing_done"), m - 1)
                if type(bt) is int and m == 0:
                    dve.wait_ge(sem("v_rstd"), 1)
                for n in range(TB):
                    dve.tensor_scalar(tmp[:, 2 + j % 2, P * n:P * (n + 1)], work[:, m, P * n:P * (n + 1)],
                                      self.mean_var[:, n, 0:1], self.v_rstd[:, n:n + 1], ALU.subtract,
                                      ALU.mult).then_inc(sem("v_normed"), 1)

            def mix_tensor(self, pe, bt, j):
                m = LANES * bt + j
                pe.wait_ge(sem("v_normed"), TB * (m + 1))
                if type(bt) is not int or m >= 2:
                    pe.wait_ge(sem("mixed_ready"), m - 1)
                for n in range(TB):
                    mm = pe.matmul(mix[j % 2][:, P * n:P * (n + 1)], tmp[:, 2 + j % 2, P * n:P * (n + 1)],
                                   self.w_turned[:, 2 * bt + j // 2, :], start=True, stop=True)
                mm.then_inc(sem("mixing_done"), 1)

            def mix_vector(self, dve, bt, j):
                m, g = LANES * bt + j, 2 * bt + j // 2
                if type(bt) is int and m == 0:
                    dve.wait_ge(sem("bs_loaded"), 16)
                else:
                    dve.wait_ge(sem("mixed_ready"), m)
                dve.scalar_tensor_tensor(q_row[:], self.row_sums[:, g, :], vecs[:, bass.ds(ROWS["gmlp_ln_b"] + m, 1)],
                                         bs_all[:, g, :], ALU.mult, ALU.add).then_inc(sem("q_row_ready"), 1)
                dve.wait_ge(sem("q_row_ready"), m + 1)
                dve.wait_ge(sem("mixing_done"), m + 1)
                t = tmp[:, 4 + j % 2, :]
                dve.scalar_tensor_tensor(t.rearrange("p (n t) -> p n t", n=TB),
                                         mix[j % 2][:].rearrange("p (n t) -> p n t", n=TB),
                                         vecs[:, bass.ds(ROWS["gmlp_ln_g"] + m, 1)],
                                         q_row[:].rearrange("p (o t) -> p o t", o=1).to_broadcast([P, TB, P]),
                                         ALU.mult, ALU.add).then_inc(sem("mixed_ready"), 1)

            def rest_vector(self, dve, bt, j):
                m, t = LANES * bt + j, tmp[:, 4 + j % 2, :]
                dve.wait_ge(sem("mix_hi"), m + 1)
                dve.tensor_tensor(act_lo[:, m, :], t, f32(act_hi[:, m, :]), ALU.subtract).then_inc(sem("mix_lo"), 1)

            def mix_pool(self, pool, bt, j):
                m = LANES * bt + j
                pool.wait_ge(sem("mixed_ready"), m + 1)
                pool.wait_ge(sem("u_ready"), m + 1)
                t = tmp[:, 4 + j % 2, :]
                pool.tensor_tensor(t, t, work[:, 24 + m, :], ALU.mult).then_inc(sem("mix_prod"), 1)

            def mix_scalar(self, act, bt, j):
                m = LANES * bt + j
                act.wait_ge(sem("mix_prod"), m + 1)
                act.activation(act_hi[:, m, :], tmp[:, 4 + j % 2, :], ACT.Copy).then_inc(sem("mix_hi"), 1)

        v_stats_sb = sb("v_stats_sb", [P, TB, 4, 6])
        in_phases = [i for i, (kind, _) in enumerate(phases) if kind.endswith("_in")]
        mixes = {}
        for i, (kind, ph) in enumerate(phases):
            if kind == "hgrn_in":
                mixes[i] = (Attention(0, ph, 0, 24), Hgrn(ph))
            if kind == "gmlp_in":
                mixes[i] = (Attention(1, ph, 24, 32), Gmlp(ph))

        block = ctx.enter_context(nc.Block())

        @block.sync
        def _(sp):
            for mb in range(MB):
                sp.dma_start(mem_raw[:, mb, :], a["mem"][0, mb * P:(mb + 1) * P, :]).then_inc(sem(f"mem_loaded{mb}"), 16)

            def load(q, j, src, nkb=KU, fresh=False):
                if not fresh:
                    sp.wait_ge(unit_done, LANES * q + j - 3)
                    stand_alone(sp)
                sp.dma_start(raw[:, j, 0:nkb, :], src).then_inc(w_loaded[j], 16)

            def cols(block):
                return bass.ds(block * P, P)

            for layer in range(2):
                def kv_body(it, fresh=False):
                    for j in range(LANES):
                        if fresh and j == 3:
                            sp.dma_start(x_raw, a["x"][0].rearrange("(tb p) c -> p tb c", p=P)).then_inc(sem("x_loaded"), 16)
                        load(4 * layer + it, j, kv_w[layer][:, :, cols(LANES * it + j)], fresh=fresh)
                if layer == 0:
                    kv_body(0, fresh=True)
                loop(sp, 1 - layer, 4, kv_body)

            n_ffn = 0
            for kind, ph in phases:
                if kind == "ffn_in":
                    w = ffn_w[n_ffn][0]

                    def body(it):
                        for j in range(LANES):
                            load(ph.q0 + it, j, w[:, :, cols((j % 2) * FB + 2 * it + j // 2)])
                    loop(sp, 0, FB // 2, body)
                elif kind == "hgrn_in":
                    w = hgrn_w[0]

                    def body(it):
                        for j in range(LANES):
                            load(ph.q0 + it, j, w[:, :, cols(4 * DB + LANES * it + j)])
                    loop(sp, 0, 2, body)

                    def body(h):
                        for j in range(LANES):
                            load(ph.q0 + 2 + h, j, w[:, :, cols(DB * j + h)])
                    loop(sp, 0, HEADS, body)
                elif kind == "gmlp_in":
                    w = gmlp_w[0]
                    for first_quad, quads, at in ((0, 2, 2 * GB), (2, 4, GB), (6, 4, 0)):
                        def body(it):
                            for j in range(LANES):
                                load(ph.q0 + first_quad + it, j, w[:, :, cols(at + LANES * it + j)])
                        loop(sp, 0, quads, body)
                else:
                    w = (ffn_w[n_ffn] if kind == "ffn_out" else hgrn_w if kind == "hgrn_out" else gmlp_w)[1]
                    rows = OUT_ROWS[kind]

                    def body(it):
                        for r, (w0, _, nkb) in enumerate(rows):
                            for g in range(LANES):
                                load(ph.q0 + len(rows) * it + r, g, w[:, w0:w0 + nkb, cols(LANES * it + g)], nkb)
                    loop(sp, 0, 2, body)
                    n_ffn += kind == "ffn_out"
            out_v = out[0].rearrange("(tb p) c -> p tb c", p=P)
            for tb in range(TB):
                sp.wait_ge(sem("rows_by_vector" if tb % 2 == 0 else "rows_by_scalar"), tb // 2 + 1)
                sp.dma_start(out_v[:, tb, :], out_rows[:, tb, :]).then_inc(sem("stored"), 16)
            sp.wait_ge(sem("stored"), 16 * TB)

        @block.tensor
        def _(pe):
            pe.wait_ge(sem("consts"), 4)
            for mb in range(MB):
                pe.wait_ge(sem(f"mem_loaded{mb}"), 16)
                for kb in range(DB):
                    m = pe.transpose(mix[kb // 2][:, (kb % 2) * MEM + mb * P:(kb % 2) * MEM + (mb + 1) * P],
                                     mem_raw[:, mb, kb * P:(kb + 1) * P], ident[:])
                    if mb == MB - 1 and kb % 2:
                        m.then_inc(sem("mem_turned"), 1)
            pe.wait_ge(sem("gain_loaded"), 16)
            pe.transpose(acc[2][:, 0:DB], vec_rows[0:DB, :], ident[0:DB, 0:DB]).then_inc(sem("vecs_turned"), 1)

            def turn_vectors():
                pe.wait_ge(sem("mem_rstd_wide"), MB)
                for mb in range(MB):
                    pe.matmul(acc[3][:, mb * P:(mb + 1) * P], tmp[:, 5, mb * P:(mb + 1) * P], ident[:], start=True,
                              stop=True)
                pe.wait_ge(sem("rows_loaded"), 16 * (len(VECTORS) - 1))
                pe.transpose(acc[3][:, MEM:MEM + NROWS], vec_rows[0:NROWS, :],
                             ident[0:NROWS, 0:NROWS]).then_inc(sem("vecs_turned"), 1)

            def turn_x(u):
                if u == 0:
                    pe.wait_ge(sem("x_loaded"), 16)
                if u >= 2:
                    pe.wait_ge(sem("x_ready"), u - 1)
                for tb in range(TB):
                    m = pe.transpose(mix[2 + u % 2][:, tb * P:(tb + 1) * P], x_raw[:, tb, u * P:(u + 1) * P], ident[:])
                m.then_inc(sem("x_turned"), 1)

            def unit(q, j, operands, bank, start, stop, each=None):
                pe.wait_ge(w_lo_ready, LANES * q + j + 1)
                last = len(operands) - 1
                for i, (hi, lo) in enumerate(operands):
                    if each:
                        each(i)
                    pe.matmul(bank, w_hi[:, j, i, :], hi, start=(start and i == 0), stop=False)
                    pe.matmul(bank, w_hi[:, j, i, :], lo, start=False, stop=False)
                    m = pe.matmul(bank, w_lo[:, j, i, :], hi, start=False, stop=(stop and i == last))
                m.then_inc(unit_done, 1)

            mem_parts = [(mem_hi[:, k, :], mem_lo[:, k, :]) for k in range(DB)]

            def mem_block(k):
                pe.wait_ge(sem("mem_lo_ready"), k // 2 + 1)

            def kv_turn(q, j, first=False):
                n = LANES * q + j
                pe.wait_ge(acc_read, n + 1)
                if not (first and j < 2):
                    pe.wait_ge(sem("v_staged"), n - 1)
                for mb in range(MB):
                    m = pe.transpose(mix[j % 2][:, mb * P:(mb + 1) * P], tmp[:, j, mb * P:(mb + 1) * P], ident[:])
                m.then_inc(sem("kv_turned"), 1)

            def kv_body(it, first=False):
                for j in range(LANES):
                    if first and j == 2:
                        pe.wait_ge(sem("vecs_ready"), 1)
                    if first and j == 3:
                        pe.wait_ge(sem("vecs_ready"), 2)
                    if not first:
                        pe.wait_ge(acc_read, LANES * it + j - 3)
                    unit(it, j, mem_parts, acc[j][:, 0:MEM], True, True, mem_block if first and j == 0 else None)
                    if first and j == 1:
                        turn_vectors()
                    if j:
                        kv_turn(it, j - 1, first)
                    elif not first:
                        kv_turn(it - 1, 3)
                    if type(it) is int and it < 2:
                        turn_x(LANES * it + j)

            kv_body(0, first=True)
            kv_body(1)
            loop(pe, 2, 8, kv_body)
            kv_turn(7, 3)

            h_parts = [(h_hi[:, k, :], h_lo[:, k, :]) for k in range(DB)]

            def in_unit(ph, s, it, j, first=False):
                def each(i):
                    pe.wait_ge(h_lo_ready, DB * s + i + 1)
                pe.wait_ge(acc_read, ph.g0 + LANES * it + j - 3)
                unit(ph.q0 + it, j, h_parts, acc[j][:], True, True, each if first and j == 0 else None)
                if first and j == 0:
                    if s == 0:
                        pe.wait_ge(sem("v_staged"), 32)
                    pe.wait_ge(sq_sum_ready, DB * (s + 1))
                    pe.matmul(mix[3][:], ones[:], sq_sum, start=True, stop=True).then_inc(ss_done, 1)

            s = n_ffn = 0
            for i, (kind, ph) in enumerate(phases):
                if kind == "ffn_in":
                    def body(it, first=False):
                        for j in range(LANES):
                            in_unit(ph, s, it, j, first)
                    body(0, first=True)
                    loop(pe, 1, FB // 2, body)
                elif kind == "hgrn_in":
                    att, hg = mixes[i]
                    for u in range(12):
                        in_unit(ph, s, u // LANES, u % LANES, first=(u == 0))
                        att.tensor(pe, u)

                    def body(h, finish=True):
                        for j in range(LANES):
                            in_unit(ph, s, 2 + h, j)
                            hg.tensor(pe, h, j, finish)
                    body(1, finish=False)
                    loop(pe, 2, HEADS, body)
                elif kind == "gmlp_in":
                    att, gm = mixes[i]
                    for u in range(12):
                        in_unit(ph, s, u // LANES, u % LANES, first=(u == 0))
                        gm.setup_tensor(pe, u)
                        if u >= 8:
                            gm.v_tensor(pe, 0, u - 8, first=True)
                        att.tensor(pe, u)

                    def v_body(it):
                        for j in range(LANES):
                            in_unit(ph, s, 2 + it, j)
                            gm.v_tensor(pe, it, j)
                    loop(pe, 1, 4, v_body)
                    for j in range(LANES):
                        in_unit(ph, s, 6, j)
                        if j == 0:
                            gm.v_tensor(pe, 4, 0)

                    def u_body(it):
                        for j in range(LANES):
                            in_unit(ph, s, 6 + it, j)
                            gm.mix_tensor(pe, it - 1, j)
                    u_body(1)
                    loop(pe, 2, 4, u_body)
                else:
                    rows = OUT_ROWS[kind]

                    def body(it, beside=None):
                        for r, (_, a0, nkb) in enumerate(rows):
                            parts = [(act_hi[:, a0 + k, :], act_lo[:, a0 + k, :]) for k in range(nkb)]
                            for g in range(LANES):
                                def each(k):
                                    if kind == "ffn_out":
                                        pe.wait_ge(act_lo_ready, FB * n_ffn + a0 + k + 1)
                                    elif a0 == 16:
                                        pe.wait_ge(sem("o_mem_lo"), 2 * XH * (n_ffn // 2 + 1))
                                    elif kind == "hgrn_out":
                                        pe.wait_ge(sem("o_lo"), k + 1)
                                    else:
                                        pe.wait_ge(sem("mix_lo"), a0 + k + 1)
                                if r == 0:
                                    pe.wait_ge(acc_read, ph.g0 + LANES * it + g - 3)
                                unit(ph.q0 + len(rows) * it + r, g, parts, acc[g][:], r == 0, r == len(rows) - 1,
                                     each if g == 0 and (beside is not None or kind == "ffn_out") else None)
                                if beside and r == 0:
                                    beside(g)
                                if s == len(in_phases) and r == len(rows) - 1:
                                    turn_out(it, g)

                    def turn_out(it, g):
                        for gg in ([g - 1] if g else []) + ([g] if g == LANES - 1 else []):
                            m_ = LANES * it + gg
                            pe.wait_ge(xg_ready, DB * s + m_ + 1)
                            for tb in range(TB):
                                m = pe.transpose(mix[gg][:, tb * P:(tb + 1) * P], tmp[:, 4 + gg % 2, tb * P:(tb + 1) * P],
                                                 ident[:])
                            m.then_inc(sem("out_turned"), 1)

                    s += 1
                    if kind == "hgrn_out":
                        hg = mixes[i - 1][1]
                        body(0, beside=lambda g: hg.tensor(pe, HEADS, g, True))
                        body(1)
                    elif kind == "gmlp_out":
                        gm = mixes[i - 1][1]
                        body(0, beside=lambda g: gm.mix_tensor(pe, 3, g))
                        body(1)
                    else:
                        if s == len(in_phases):
                            body(0)
                            pe.wait_ge(sem("out_staged"), LANES)
                            body(1)
                        else:
                            loop(pe, 0, 2, body)
                        n_ffn += 1
                    continue
            pe.wait_ge(sq_sum_ready, DB * (s + 1))
            pe.wait_ge(acc_read, Phase.group)
            for tb in range(TB):
                m = pe.matmul(acc[0][:, tb:tb + 1], sq_sum[:, tb * P:(tb + 1) * P], ones[:, 0:1], start=True, stop=True)
            m.then_inc(ss_done, 1)

        @block.vector
        def _(dve):
            def lo(q, j, nkb=KU):
                dve.wait_ge(w_hi_ready, LANES * q + j + 1)
                dve.tensor_tensor(w_lo[:, j, 0:nkb], raw[:, j, 0:nkb], f32(w_hi[:, j, 0:nkb]), ALU.subtract).then_inc(w_lo_ready, 1)

            dve.wait_ge(sem("vecs_turned"), 1)
            dve.tensor_copy(vecs[:, 0:DB], acc[2][:, 0:DB]).then_inc(sem("vecs_ready"), 1)
            dve.wait_ge(sem("vecs_ready"), 1)

            def mem_rest(n):
                pr = slice(2 * n, 2 * n + 2)
                dve.wait_ge(sem("mem_hi_ready"), n + 1)
                dve.tensor_tensor(mem_lo[:, pr, :], mem_g[:, pr, :], f32(mem_hi[:, pr, :]),
                                  ALU.subtract).then_inc(sem("mem_lo_ready"), 1)
            for kb in range(DB):
                dve.wait_ge(sem("mem_turned"), kb // 2 + 1)
                g = ROWS["mem_norm"] + kb
                dve.tensor_scalar(mem_g[:, kb, :], mix[kb // 2][:, (kb % 2) * MEM:(kb % 2 + 1) * MEM], vecs[:, g:g + 1],
                                  None, ALU.mult).then_inc(sem("mem_gained"), 1)
                if kb == 3:
                    lo(0, 0)
                    mem_rest(0)
            for n in range(1, DB // 2):
                mem_rest(n)
            lo(0, 1)
            mss = small[:, 60:62]
            dve.wait_ge(sem("mem_squared"), MB)
            dve.tensor_scalar(mss, mss, 1.0 / D, EPS, ALU.mult, ALU.add).then_inc(sem("mem_var"), 1)
            dve.wait_ge(sem("mem_std"), 1)
            dve.reciprocal(mss, mss).then_inc(sem("mem_rstd"), 1)
            dve.wait_ge(sem("mem_rstd"), 1)
            for mb in range(MB):
                dve.tensor_scalar(tmp[:, 5, mb * P:(mb + 1) * P], ones[:], mss[:, mb:mb + 1], None,
                                  ALU.mult).then_inc(sem("mem_rstd_wide"), 1)
            lo(0, 2)
            dve.wait_ge(sem("vecs_turned"), 2)
            dve.tensor_copy(rstd[:, 0:MEM], acc[3][:, 0:MEM]).then_inc(sem("mem_rstd_ready"), 1)
            dve.tensor_copy(vecs[:], acc[3][:, MEM:MEM + NROWS]).then_inc(sem("vecs_ready"), 1)
            dve.wait_ge(sem("mem_rstd_ready"), 1)

            def take_x(u):
                dve.wait_ge(sem("x_turned"), u + 1)
                dve.tensor_copy(x[:, u, :], mix[2 + u % 2][:]).then_inc(sem("x_ready"), 1)
            def lower_bounds():
                lg = [vecs[:, ROWS["lb_logits"] + DB * i:ROWS["lb_logits"] + DB * (i + 1)] for i in range(3)]
                top, e = small[:, 64:72], [small[:, 72 + 8 * i:80 + 8 * i] for i in range(3)]
                dve.tensor_tensor(top, lg[0], lg[1], ALU.max).then_inc(sem("lb_step"), 1)
                dve.wait_ge(sem("lb_step"), 1)
                dve.tensor_tensor(top, top, lg[2], ALU.max).then_inc(sem("lb_step"), 1)
                dve.wait_ge(sem("lb_step"), 2)
                for i in range(3):
                    dve.tensor_tensor(e[i], lg[i], top, ALU.subtract).then_inc(sem("lb_shifted"), 1)
                dve.wait_ge(sem("lb_exp"), 1)
                dve.tensor_tensor(top, e[0], e[1], ALU.add).then_inc(sem("lb_step"), 1)
                dve.wait_ge(sem("lb_step"), 3)
                dve.tensor_tensor(top, top, e[2], ALU.add).then_inc(sem("lb_step"), 1)
                dve.wait_ge(sem("lb_step"), 4)
                dve.reciprocal(top, top).then_inc(sem("lb_step"), 1)
                dve.wait_ge(sem("lb_step"), 5)
                dve.tensor_tensor(small[:, 24:32], e[0], top, ALU.mult).then_inc(sem("lb_step"), 1)
                dve.wait_ge(sem("lb_step"), 6)
                dve.tensor_scalar(small[:, 32:40], small[:, 24:32], -1.0, 1.0, ALU.mult, ALU.add).then_inc(sem("lb_step"), 1)
                dve.wait_ge(sem("lb_step"), 7)

            def gained(s, m_, t):
                g = GAINS[s] + m_
                dve.tensor_scalar(t, x[:, m_, :], vecs[:, bass.ds(g, 1)], None, ALU.mult).then_inc(xg_ready, 1)

            def h_rest(s, m_, t):
                dve.wait_ge(h_hi_ready, DB * s + m_ + 1)
                dve.tensor_tensor(h_lo[:, m_, :], t, f32(h_hi[:, m_, :]), ALU.subtract).then_inc(h_lo_ready, 1)

            def kv_body(it, first=False):
                def take(j):
                    dve.wait_ge(unit_done, LANES * it + j + 1)
                    if not first:
                        dve.wait_ge(sem(f"k_stored{j}"), 16 * it)
                        dve.wait_ge(sem("kv_turned"), LANES * it + j - 3)
                    dve.tensor_tensor(tmp[:, j, 0:MEM], acc[j][:, 0:MEM], rstd[:, 0:MEM], ALU.mult).then_inc(acc_read, 1)
                    if type(it) is int and it < 2:
                        take_x(LANES * it + j)
                for j in range(LANES):
                    if first and j == 1:
                        lo(0, 3)
                    if j:
                        take(j - 1)
                    if j == 1:
                        dve.wait_ge(sem("x_ready"), it + 1)
                        gained(0, it, tmp[:, 4, :])
                    if j == 2:
                        h_rest(0, it, tmp[:, 4, :])
                    if not (first and j < 2):
                        lo(*ahead(it, j))
                take(3)

            kv_body(0, first=True)
            kv_body(1)
            lower_bounds()
            loop(dve, 2, 8, kv_body)

            def norm_stats(s):
                dve.wait_ge(ss_done, s + 1)
                dve.tensor_scalar(rstd[:], mix[3][:], 1.0 / D, EPS, ALU.mult, ALU.add).then_inc(var_ready, 1)
                dve.wait_ge(std_ready, s + 1)
                dve.reciprocal(rstd[:], rstd[:]).then_inc(rstd_ready, 1)
                dve.wait_ge(rstd_ready, s + 1)

            s = n_ffn = 0
            for i, (kind, ph) in enumerate(phases):
                if kind == "ffn_in":
                    if i == 0:
                        for j in range(LANES):
                            dve.wait_ge(sem(f"k_stored{j}"), 16 * 8)
                            dve.wait_ge(sem(f"kv_stored{j}"), 16 * 8)

                    def body(it, first=False):
                        f0 = FB * n_ffn + 2 * it

                        def gate(j):
                            dve.wait_ge(unit_done, LANES * (ph.q0 + it) + j + 1)
                            dve.tensor_tensor(tmp[:, j, :], acc[j][:], rstd[:], ALU.mult).then_inc(acc_read, 1)

                        def up(j):
                            gate(j)
                            dve.wait_ge(acc_read, ph.g0 + LANES * it + j + 1)
                            dve.wait_ge(silu_done, f0 + j // 2 + 1)
                            dve.tensor_tensor(tmp[:, j, :], tmp[:, j, :], tmp[:, j - 1, :], ALU.mult).then_inc(prod_done, 1)

                        def rest(j):
                            f = 2 * it + j // 2
                            dve.wait_ge(act_hi_ready, f0 + j // 2 + 1)
                            dve.tensor_tensor(act_lo[:, f, :], tmp[:, j, :], f32(act_hi[:, f, :]),
                                              ALU.subtract).then_inc(act_lo_ready, 1)
                        lo(ph.q0 + it, 2)
                        if first:
                            norm_stats(s)
                        gate(0)
                        lo(ph.q0 + it, 3)
                        up(1)
                        lo(ph.q0 + it + 1, 0)
                        rest(1)
                        gate(2)
                        lo(ph.q0 + it + 1, 1)
                        up(3)
                        rest(3)
                    body(0, first=True)
                    loop(dve, 1, FB // 2, body)
                elif kind == "hgrn_in":
                    att, hg = mixes[i]
                    for u in range(12):
                        if u == 1:
                            norm_stats(s)
                        att.vector(dve, u)
                        if u >= 8:
                            hg.vector(dve, 0, u - 8, True, False, False)
                        lo(*ahead(ph.q0 + u // LANES, u % LANES))

                    def body(h, finish=True):
                        for j in range(LANES):
                            hg.vector(dve, h, j, True, True, finish)
                            lo(*ahead(ph.q0 + 2 + h, j))
                    body(1, finish=False)
                    loop(dve, 2, HEADS, body)
                elif kind == "gmlp_in":
                    att, gm = mixes[i]
                    for u in range(12):
                        if u == 1:
                            norm_stats(s)
                        gm.setup_vector(dve, u)
                        att.vector(dve, u)
                        if u >= 8:
                            gm.v_vector(dve, 0, u - 8, first=True)
                        lo(*ahead(ph.q0 + u // LANES, u % LANES))

                    def v_body(it):
                        for j in range(LANES):
                            gm.v_vector(dve, it, j)
                            gm.v_stats(dve, it, j)
                            lo(*ahead(ph.q0 + 2 + it, j))
                    loop(dve, 1, 4, v_body)
                    for j in range(LANES):
                        if j == 0:
                            gm.v_vector(dve, 4, 0)
                        else:
                            gm.u_vector(dve, 0, j - 1)
                        gm.v_stats(dve, 4, j)
                        lo(*ahead(ph.q0 + 6, j))
                    gm.v_stats_end(dve)
                    gm.u_vector(dve, 0, 3)

                    def u_body(it, first=False):
                        for j in range(LANES):
                            gm.norm_vector(dve, it - 1, j)
                            if j:
                                gm.u_vector(dve, it, j - 1)
                                gm.mix_vector(dve, it - 1, j - 1)
                            elif not first:
                                gm.u_vector(dve, it - 1, 3)
                                gm.mix_vector(dve, it - 2, 3)
                            lo(*ahead(ph.q0 + 6 + it, j))
                            if j:
                                gm.rest_vector(dve, it - 1, j - 1)
                            elif not first:
                                gm.rest_vector(dve, it - 2, 3)
                    u_body(1, first=True)
                    loop(dve, 2, 4, u_body)
                else:
                    rows = OUT_ROWS[kind]
                    nr = len(rows)
                    scale = 0.5 if kind == "ffn_out" else 1.0
                    s += 1
                    final = s == len(in_phases)

                    def body(it, beside=None, last=False):
                        def take(g):
                            m_, t = LANES * it + g, tmp[:, 4 + g % 2, :]
                            dve.wait_ge(unit_done, LANES * (ph.q0 + nr * it + nr - 1) + g + 1)
                            dve.scalar_tensor_tensor(x[:, m_, :], acc[g][:], scale, x[:, m_, :], ALU.mult,
                                                     ALU.add).then_inc(acc_read, 1)
                            dve.wait_ge(acc_read, ph.g0 + m_ + 1)
                            if final and m_ >= 2:
                                dve.wait_ge(sem("out_turned"), m_ - 1)
                            gained(s, m_, t)
                            if not final:
                                h_rest(s, m_, t)
                        for r in range(nr):
                            for g in range(LANES):
                                if beside:
                                    beside(LANES * r + g)
                                if r == nr - 1 and g:
                                    take(g - 1)
                                if not (last and r == nr - 1 and g >= 2):
                                    lo(*ahead(ph.q0 + nr * it + r, g), blocks_ahead(kind, r, g))
                        take(3)
                    if kind == "hgrn_out":
                        hg = mixes[i - 1][1]

                        def beside(u):
                            if u < LANES:
                                hg.vector(dve, HEADS, u, False, True, True)
                            if u == LANES:
                                hg.vector(dve, HEADS + 1, 0, False, False, True)
                        body(0, beside)
                        body(1)
                    elif kind == "gmlp_out":
                        gm = mixes[i - 1][1]

                        def beside(u):
                            if u < LANES:
                                gm.norm_vector(dve, 3, u)
                            if u == 0:
                                gm.u_vector(dve, 3, 3)
                                gm.mix_vector(dve, 2, 3)
                                gm.rest_vector(dve, 2, 3)
                            if 1 <= u <= LANES:
                                gm.mix_vector(dve, 3, u - 1)
                                gm.rest_vector(dve, 3, u - 1)
                        body(0, beside)
                        body(1)
                    else:
                        if final:
                            body(0)
                            body(1, last=True)
                        else:
                            loop(dve, 0, 2, body)
                        n_ffn += 1
            fin = small[:, 44:48]
            dve.wait_ge(ss_done, s + 1)
            dve.tensor_scalar(fin, acc[0][:, 0:TB], 1.0 / D, EPS, ALU.mult, ALU.add).then_inc(var_ready, 1)
            dve.wait_ge(std_ready, s + 1)
            dve.reciprocal(fin, fin).then_inc(rstd_ready, 1)
            dve.wait_ge(rstd_ready, s + 1)
            dve.wait_ge(sem("out_staged"), DB)
            for tb in (0, 2):
                dve.tensor_scalar(out_rows[:, tb, :], out_rows[:, tb, :], fin[:, tb:tb + 1], None,
                                  ALU.mult).then_inc(sem("rows_by_vector"), 1)

        @block.scalar
        def _(act):
            act.dma_start(vec_rows[0:DB, :], a["mem_norm"].rearrange("(r c) -> r c", c=P)).then_inc(sem("gain_loaded"), 16)
            act.preload_act_table(ACT.Sqrt)

            def hi(q, j, nkb=KU):
                act.wait_ge(w_loaded[j], 16 * (q + 1))
                act.activation(w_hi[:, j, 0:nkb], raw[:, j, 0:nkb], ACT.Copy).then_inc(w_hi_ready, 1)

            hi(0, 0)
            for n in range(DB // 2):
                pr = slice(2 * n, 2 * n + 2)
                act.wait_ge(sem("mem_gained"), 2 * n + 2)
                act.activation(mem_hi[:, pr, :], mem_g[:, pr, :], ACT.Copy).then_inc(sem("mem_hi_ready"), 1)
            hi(0, 1)
            for mb in range(MB):
                act.wait_ge(sem(f"mem_loaded{mb}"), 16)
                act.activation(mem_junk, mem_raw[:, mb, :], ACT.Square,
                               accum_out=small[:, 60 + mb:61 + mb]).then_inc(sem("mem_squared"), 1)
                act.wait_ge(sem("mem_squared"), mb + 1)
            act.wait_ge(sem("mem_var"), 1)
            act.activation(small[:, 60:62], small[:, 60:62], ACT.Sqrt).then_inc(sem("mem_std"), 1)

            def h_top(s, m_, t):
                act.wait_ge(xg_ready, DB * s + m_ + 1)
                act.activation(h_hi[:, m_, :], t, ACT.Copy).then_inc(h_hi_ready, 1)

            def kv_body(it, first=False):
                def take(q, j, first):
                    act.wait_ge(sem("kv_turned"), LANES * q + j + 1)
                    if not first:
                        act.wait_ge(sem(f"kv_stored{j}"), 16 * q)
                    act.activation(tmp[:, j, MEM:2 * MEM], mix[j % 2][:, 0:MEM], ACT.Copy).then_inc(sem("v_staged"), 1)
                for j in range(LANES):
                    if first and j == 1:
                        hi(0, 3)
                    if j == 1:
                        h_top(0, it, tmp[:, 4, :])
                        if not first:
                            take(it - 1, 3, type(it) is int and it == 1)
                    if j >= 2:
                        take(it, j - 2, first)
                    if not (first and j == 1):
                        hi(*ahead(it, j))
                take(it, 2, first)

            kv_body(0, first=True)
            kv_body(1)
            act.wait_ge(sem("lb_shifted"), 3)
            act.activation(small[:, 72:96], small[:, 72:96], ACT.Exp).then_inc(sem("lb_exp"), 1)
            loop(act, 2, 8, kv_body)
            act.wait_ge(sem("kv_turned"), 32)
            act.wait_ge(sem("kv_stored3"), 16 * 7)
            act.activation(tmp[:, 3, MEM:2 * MEM], mix[1][:, 0:MEM], ACT.Copy).then_inc(sem("v_staged"), 1)

            def root(s):
                act.wait_ge(var_ready, s + 1)
                act.activation(rstd[:], rstd[:], ACT.Sqrt).then_inc(std_ready, 1)

            s = n_ffn = 0
            for i, (kind, ph) in enumerate(phases):
                if kind == "ffn_in":
                    def body(it, first=False):
                        f0 = FB * n_ffn + 2 * it

                        def silu(j):
                            act.wait_ge(acc_read, ph.g0 + LANES * it + j + 1)
                            act.activation(tmp[:, j, :], tmp[:, j, :], ACT.Silu).then_inc(silu_done, 1)

                        def top(j):
                            act.wait_ge(prod_done, f0 + j // 2 + 1)
                            act.activation(act_hi[:, 2 * it + j // 2, :], tmp[:, j, :], ACT.Copy).then_inc(act_hi_ready, 1)
                        hi(ph.q0 + it, 2)
                        if first:
                            root(s)
                        silu(0)
                        hi(ph.q0 + it, 3)
                        top(1)
                        hi(ph.q0 + it + 1, 0)
                        silu(2)
                        hi(ph.q0 + it + 1, 1)
                        top(3)
                    body(0, first=True)
                    loop(act, 1, FB // 2, body)
                elif kind == "hgrn_in":
                    att, hg = mixes[i]
                    for u in range(12):
                        if u == 1:
                            root(s)
                            act.preload_act_table_set("natural_log_exp_and_others")
                        att.scalar(act, u)
                        if u >= 8:
                            hg.scalar(act, 0, u - 8, True, False, False)
                        hi(*ahead(ph.q0 + u // LANES, u % LANES))

                    def body(h, finish=True):
                        for j in range(LANES):
                            hg.scalar(act, h, j, True, True, finish)
                            hi(*ahead(ph.q0 + 2 + h, j))
                    body(1, finish=False)
                    loop(act, 2, HEADS, body)
                elif kind == "gmlp_in":
                    att, gm = mixes[i]
                    for u in range(12):
                        if u == 1:
                            root(s)
                        att.scalar(act, u)
                        if u >= 8:
                            gm.v_scalar(act, 0, u - 8, first=True)
                        hi(*ahead(ph.q0 + u // LANES, u % LANES))

                    def v_body(it):
                        for j in range(LANES):
                            gm.v_scalar(act, it, j)
                            hi(*ahead(ph.q0 + 2 + it, j))
                    loop(act, 1, 4, v_body)
                    for j in range(LANES):
                        if j == 0:
                            gm.v_scalar(act, 4, 0)
                        else:
                            if j == 1:
                                act.wait_ge(sem("v_blk_turned"), GB)
                                act.activation(work[:, GB - 1, :], mix[1][:], ACT.Copy).then_inc(sem("v_stored"), 1)
                            gm.u_scalar(act, 0, j - 1)
                        hi(*ahead(ph.q0 + 6, j))
                    act.wait_ge(sem("v_var"), 1)
                    act.activation(gm.v_rstd, gm.v_rstd, ACT.Sqrt).then_inc(sem("v_std"), 1)
                    gm.u_scalar(act, 0, 3)

                    def u_body(it, first=False):
                        for j in range(LANES):
                            if j:
                                gm.u_scalar(act, it, j - 1)
                            elif not first:
                                gm.u_scalar(act, it - 1, 3)
                            hi(*ahead(ph.q0 + 6 + it, j))
                            if j:
                                gm.mix_scalar(act, it - 1, j - 1)
                            elif not first:
                                gm.mix_scalar(act, it - 2, 3)
                    u_body(1, first=True)
                    loop(act, 2, 4, u_body)
                else:
                    nr = len(OUT_ROWS[kind])
                    s += 1
                    final = s == len(in_phases)

                    def body(it, beside=None, last=False):
                        def take(g):
                            m_, t = LANES * it + g, tmp[:, 4 + g % 2, :]
                            if not final:
                                h_top(s, m_, t)
                            else:
                                act.wait_ge(sem("out_turned"), m_ + 1)
                                act.activation(out_rows[:, :, m_ * P:(m_ + 1) * P],
                                               mix[g][:].rearrange("p (tb c) -> p tb c", tb=TB),
                                               ACT.Copy).then_inc(sem("out_staged"), 1)
                        for r in range(nr):
                            for g in range(LANES):
                                if beside:
                                    beside(LANES * r + g)
                                late = 2 if final else 1
                                if r == nr - 1 and g >= late:
                                    take(g - late)
                                if not (last and r == nr - 1 and g >= 2):
                                    hi(*ahead(ph.q0 + nr * it + r, g), blocks_ahead(kind, r, g))
                        if final:
                            take(2)
                        take(3)
                    if kind == "hgrn_out":
                        hg = mixes[i - 1][1]

                        def beside(u):
                            if u < LANES:
                                hg.scalar(act, HEADS, u, False, True, True)
                            if u == LANES:
                                hg.scalar(act, HEADS + 1, 0, False, False, True)
                        body(0, beside)
                        body(1)
                    elif kind == "gmlp_out":
                        gm = mixes[i - 1][1]

                        def beside(u):
                            if u == 0:
                                gm.u_scalar(act, 3, 3)
                                gm.mix_scalar(act, 2, 3)
                            elif u <= LANES:
                                gm.mix_scalar(act, 3, u - 1)
                        body(0, beside)
                        body(1)
                    else:
                        if final:
                            body(0)
                            body(1, last=True)
                        else:
                            loop(act, 0, 2, body)
                        n_ffn += 1
            fin = small[:, 44:48]
            act.wait_ge(var_ready, s + 1)
            act.activation(fin, fin, ACT.Sqrt).then_inc(std_ready, 1)
            act.wait_ge(rstd_ready, s + 1)
            for tb in (1, 3):
                act.activation(out_rows[:, tb, :], out_rows[:, tb, :], ACT.Copy,
                               scale=fin[:, tb:tb + 1]).then_inc(sem("rows_by_scalar"), 1)

        @block.gpsimd
        def _(pool):
            pool.memset(ident[:], 0.0).then_inc(sem("consts"), 1)
            pool.memset(ones[:], 1.0).then_inc(sem("consts"), 1)
            pool.wait_ge(sem("consts"), 2)
            pool.affine_select(out=ident[:], in_=ident[:], compare_op=ALU.not_equal, fill=1.0, base=0,
                               pattern=[[-1, P]], channel_multiplier=1).then_inc(sem("consts"), 1)
            pool.memset(small[:, 40:41], EPS).then_inc(sem("consts"), 1)
            at = DB
            for name, n in VECTORS[1:]:
                v = a[name]
                flat = v if len(v.shape) == 1 else v.rearrange("l c -> (l c)")
                pool.dma_start(vec_rows[at:at + n, :], flat.rearrange("(r c) -> r c", c=P)).then_inc(sem("rows_loaded"), 16)
                at += n
            mask, restart = pair[:, 0, :].bitcast(I32), pair[:, 1, :]
            pool.memset(mask, 1).then_inc(sem("masks"), 1)
            pool.memset(restart, 1.0).then_inc(sem("masks"), 1)
            pool.memset(sq_sum, 0.0).then_inc(sem("masks"), 1)
            pool.wait_ge(sem("masks"), 3)
            m4 = mask.rearrange("p (n t) -> p n t", n=TB)
            pool.affine_select(out=m4, in_=m4, compare_op=ALU.is_ge, fill=0, base=0, pattern=[[0, TB], [1, P]],
                               channel_multiplier=-1).then_inc(sem("masks"), 1)
            pool.wait_ge(sem("masks"), 4)
            late = m4[:, :, CHUNK:P]
            pool.affine_select(out=late, in_=late, compare_op=ALU.is_ge, fill=0, base=-CHUNK,
                               pattern=[[0, TB], [0, CHUNK]], channel_multiplier=1).then_inc(sem("masks"), 1)
            pool.memset(restart.rearrange("p (c t) -> p c t", t=CHUNK)[:, :, 0:1], 0.0).then_inc(sem("masks"), 1)

            def squares(s, m_, source, count):
                pool.wait_ge(source, count)
                if not (type(m_) is int and m_ == 0 and s == 0):
                    pool.wait_ge(sq_sum_ready, DB * s + m_)
                pool.tensor_tensor(sq_one, x[:, m_, :], x[:, m_, :], ALU.mult).then_inc(sq_ready, 1)
                pool.wait_ge(sq_ready, DB * s + m_ + 1)
                pool.tensor_tensor(sq_sum, sq_sum, sq_one, ALU.add).then_inc(sq_sum_ready, 1)

            def store_k(q, j):
                pool.wait_ge(acc_read, LANES * q + j + 1)
                stand_alone(pool)
                pool.dma_start(k_scratch[LANES * q + j], tmp[:, j, 0:MEM]).then_inc(sem(f"k_stored{j}"), 16)

            def store_v(q, j):
                pool.wait_ge(sem("v_staged"), LANES * q + j + 1)
                stand_alone(pool)
                pool.dma_start(v_scratch[LANES * q + j], tmp[:, j, MEM:2 * MEM]).then_inc(sem(f"kv_stored{j}"), 16)

            def kv_body(it, first=False):
                for j in range(LANES):
                    if j == 3:
                        squares(0, it, sem("x_ready"), it + 1)
                    if j == 0:
                        if not first:
                            store_v(it - 1, 3)
                    store_k(it, j)
                    if j:
                        store_v(it, j - 1)
            kv_body(0, first=True)
            loop(pool, 1, 8, kv_body)
            store_v(7, 3)

            s = 0
            for i, (kind, ph) in enumerate(phases):
                if kind == "hgrn_in":
                    att, hg = mixes[i]
                    att.load(pool)
                    pool.memset(hg.a_m, 0.0).then_inc(sem("masks"), 1)
                    for j in range(LANES):
                        hg.pool(pool, 0, j, True, False, False)

                    def body(h, finish=True):
                        for j in range(LANES):
                            hg.pool(pool, h, j, True, True, finish)
                    body(1, finish=False)
                    loop(pool, 2, HEADS, body)
                    for j in range(LANES):
                        hg.pool(pool, HEADS, j, False, True, True)
                    hg.pool(pool, HEADS + 1, 0, False, False, True)
                elif kind == "gmlp_in":
                    att, gm = mixes[i]
                    att.load(pool)

                    def body(bt):
                        for j in range(LANES):
                            gm.mix_pool(pool, bt, j)
                    loop(pool, 0, 4, body)
                elif not kind.endswith("_in"):
                    if kind == "hgrn_out":
                        mixes[in_phases[4]][1].setup_pool(pool)
                    s += 1
                    pool.wait_ge(ss_done, s)
                    pool.wait_ge(sem("sq_zeroed"), s - 1) if s > 1 else None
                    if kind == "gmlp_out":
                        pool.wait_ge(sem("mix_lo"), GB)
                    pool.memset(sq_sum, 0.0).then_inc(sem("sq_zeroed"), 1)
                    pool.wait_ge(sem("sq_zeroed"), s)

                    def body(it):
                        for g in range(LANES):
                            m_ = LANES * it + g
                            squares(s, m_, acc_read, ph.g0 + m_ + 1)
                    loop(pool, 0, 2, body)


_INS = ["x", "mem", "mem_norm", "lb_logits", "ffn1_norm", "ffn1_w_in", "ffn1_w_out", "mix_norm", "mem_w_kv",
        "hgrn_w_in", "hgrn_gnorm", "hgrn_w_out", "gmlp_w_in", "gmlp_ln_g", "gmlp_ln_b", "gmlp_w_s", "gmlp_b_s",
        "gmlp_w_out", "ffn2_norm", "ffn2_w_in", "ffn2_w_out", "final_norm"]
_OUTS = [((1, T, D), "float32")]


def kernel(**inputs):
    import concourse.bacc as _bacc
    from concourse.bass_utils import run_bass_kernel_spmd as _run

    nc = _bacc.Bacc("TRN2", target_bir_lowering=False, num_devices=1)
    arrays, args = {}, {}
    for name in _INS:
        arr = np.ascontiguousarray(inputs[name])
        arrays[f"in_{name}_dram"] = arr
        args[name] = nc.dram_tensor(f"in_{name}_dram", arr.shape, mybir.dt.from_np(arr.dtype),
                                    kind="ExternalInput").ap()
    outs = []
    for i, (shape, dtype) in enumerate(_OUTS):
        dt = mybir.dt.from_np(np.dtype(dtype))
        outs.append(nc.dram_tensor(f"out_{i}_dram", shape, dt, kind="ExternalOutput").ap())
    hybrid_trunk(nc, args, outs[0])
    r = _run(nc, [arrays], core_ids=[0])
    return r.results[0]["out_0_dram"]
```
